# Optimizing a Trainium2 kernel written in Bass

```python
import math, functools
import jax, jax.numpy as jnp
from jax import lax
import numpy as np

D_MODEL = 1024
BATCH = 1
SEQ = 256
DEPTH = 2

CHUNK = 64
HEAD_DIM = 64
MIX_WIDTH = D_MODEL
A_WIDTH = 3 * MIX_WIDTH // 8
B_WIDTH = 3 * MIX_WIDTH // 8
LRU_WIDTH = MIX_WIDTH - A_WIDTH - B_WIDTH
A_HEADS = A_WIDTH // HEAD_DIM
A_KV_HEADS = 2
A_GROUP = A_HEADS // A_KV_HEADS
B_HEADS = B_WIDTH // HEAD_DIM
WINDOW = 128
WINDOW_CHUNKS = WINDOW // CHUNK
B_LEFT_CHUNKS = 8
B_BAND = (B_LEFT_CHUNKS + 1) * CHUNK
REL_CLIP = 256
LRU_BLOCKS = 4
LRU_BLOCK_W = LRU_WIDTH // LRU_BLOCKS
CONV_WIDTH = 4
LRU_C = 8.0
ROT_DIM = HEAD_DIM // 4
ROPE_THETA = 500000.0
N_MEM = 256
CROSS_HEADS = 4
CROSS_HEAD_DIM = D_MODEL // CROSS_HEADS
D_FF = ((8 * D_MODEL // 3 + 127) // 128) * 128
EPS = 1e-6
NEG_INF = -1e30
MIX_SIZES = [A_WIDTH, A_KV_HEADS * HEAD_DIM, A_KV_HEADS * HEAD_DIM,
             B_WIDTH, B_WIDTH, B_WIDTH,
             LRU_WIDTH, LRU_WIDTH]
MIX_IN = sum(MIX_SIZES)
MIX_SPLITS = [int(v) for v in np.cumsum(MIX_SIZES)[:-1]]
GROUP_SPLITS = [A_WIDTH, A_WIDTH + B_WIDTH]

kernel_name = "hymba_streaming_hybrid_block"

def rms_norm(x, g):
    xf = x.astype(jnp.float32)
    y = xf * lax.rsqrt(jnp.mean(xf * xf, axis=-1, keepdims=True) + EPS)
    return (y * g.astype(jnp.float32)).astype(x.dtype)

def swiglu(h, w_in, w_out):
    gate, up = jnp.split(h @ w_in, 2, axis=-1)
    return (jax.nn.silu(gate) * up) @ w_out

def rotary_tables(s):
    pos = jnp.arange(s, dtype=jnp.float32)
    inv_freq = ROPE_THETA ** (-jnp.arange(0, ROT_DIM, 2, dtype=jnp.float32) / ROT_DIM)
    ang = pos[:, None] * inv_freq[None, :]
    return jnp.cos(ang), jnp.sin(ang)

def apply_partial_rope(t, cos, sin):
    tr, tp = t[..., :ROT_DIM], t[..., ROT_DIM:]
    t1, t2 = jnp.split(tr.astype(jnp.float32), 2, axis=-1)
    c, s_ = cos[None, :, None, :], sin[None, :, None, :]
    rot = jnp.concatenate([t1 * c - t2 * s_, t2 * c + t1 * s_], axis=-1)
    return jnp.concatenate([rot.astype(t.dtype), tp], axis=-1)

def sliding_window_sink_attention(q, k, v, sinks):
    b, s = q.shape[:2]
    nc = s // CHUNK
    qc = q.reshape(b, nc, CHUNK, A_KV_HEADS, A_GROUP, HEAD_DIM)

    def band(t):
        tc = t.reshape(b, nc, CHUNK, A_KV_HEADS, HEAD_DIM)
        tp = jnp.pad(tc, ((0, 0), (WINDOW_CHUNKS - 1, 0), (0, 0), (0, 0), (0, 0)))
        return jnp.concatenate([tp[:, j:j + nc] for j in range(WINDOW_CHUNKS)], axis=2)

    kb, vb = band(k), band(v)
    logits = jnp.einsum('bnqhgd,bnkhd->bnhgqk', qc, kb).astype(jnp.float32) * (HEAD_DIM ** -0.5)
    valid = (jnp.arange(nc)[:, None] + jnp.arange(WINDOW_CHUNKS)[None, :] - (WINDOW_CHUNKS - 1)) >= 0
    valid = jnp.repeat(valid, CHUNK, axis=1)
    logits = jnp.where(valid[None, :, None, None, None, :], logits, NEG_INF)
    sink = sinks.astype(jnp.float32).reshape(A_KV_HEADS, A_GROUP)[None, None, :, :, None, None]
    sink = jnp.broadcast_to(sink, logits.shape[:-1] + (1,))
    probs = jax.nn.softmax(jnp.concatenate([logits, sink], axis=-1), axis=-1)[..., :-1]
    out = jnp.einsum('bnhgqk,bnkhd->bnqhgd', probs.astype(vb.dtype), vb)
    return out.reshape(b, s, A_WIDTH)

def chunk_relbias_attention(q, k, v, rel_table):
    b, s = q.shape[:2]
    nc = s // CHUNK
    left = B_LEFT_CHUNKS * CHUNK
    kp = jnp.pad(k, ((0, 0), (left, 0), (0, 0), (0, 0)))
    vp = jnp.pad(v, ((0, 0), (left, 0), (0, 0), (0, 0)))
    rel = (jnp.arange(CHUNK)[:, None] + left) - jnp.arange(B_BAND)[None, :]
    bias = rel_table.astype(jnp.float32)[:, jnp.clip(rel, -REL_CLIP, REL_CLIP) + REL_CLIP]

    def one_chunk(c):
        start = c * CHUNK
        qc = lax.dynamic_slice_in_dim(q, start, CHUNK, axis=1)
        kb = lax.dynamic_slice_in_dim(kp, start, B_BAND, axis=1)
        vb = lax.dynamic_slice_in_dim(vp, start, B_BAND, axis=1)
        logits = jnp.einsum('bqhd,bkhd->bhqk', qc, kb).astype(jnp.float32) * (HEAD_DIM ** -0.5) + bias[None]
        key_pos = start - left + jnp.arange(B_BAND)
        logits = jnp.where((key_pos >= 0)[None, None, None, :], logits, NEG_INF)
        p = jax.nn.softmax(logits, axis=-1)
        return jnp.einsum('bhqk,bkhd->bqhd', p.astype(vb.dtype), vb)

    out = lax.map(one_chunk, jnp.arange(nc))
    return out.transpose(1, 0, 2, 3, 4).reshape(b, s, B_WIDTH)

def causal_depthwise_conv(x, w, bias):
    out = lax.conv_general_dilated(
        x, w[:, None, :].astype(x.dtype), window_strides=(1,), padding=[(CONV_WIDTH - 1, 0)],
        dimension_numbers=('NWC', 'WIO', 'NWC'), feature_group_count=x.shape[-1])
    return out + bias

def rg_lru(xr, w_a, b_a, w_x, b_x, lam):
    b, s, w = xr.shape
    xh = xr.reshape(b, s, LRU_BLOCKS, LRU_BLOCK_W)
    r = jax.nn.sigmoid(jnp.einsum('bsnc,ncd->bsnd', xh, w_a).reshape(b, s, w) + b_a)
    i = jax.nn.sigmoid(jnp.einsum('bsnc,ncd->bsnd', xh, w_x).reshape(b, s, w) + b_x)
    log_a = -LRU_C * r.astype(jnp.float32) * jax.nn.softplus(-lam.astype(jnp.float32))
    a = jnp.exp(log_a)
    u = jnp.sqrt(-jnp.expm1(2.0 * log_a)) * (i * xr).astype(jnp.float32)

    def combine(lhs, rhs):
        a1, b1 = lhs
        a2, b2 = rhs
        return a1 * a2, a2 * b1 + b2

    _, h = lax.associative_scan(combine, (a, u), axis=1)
    return h.astype(xr.dtype)

def cross_attention(h, m, w_q, w_kv, w_o):
    b, s, _ = h.shape
    nm = m.shape[1]
    q = (h @ w_q).reshape(b, s, CROSS_HEADS, CROSS_HEAD_DIM)
    k, v = jnp.split(m @ w_kv, 2, axis=-1)
    k = k.reshape(b, nm, CROSS_HEADS, CROSS_HEAD_DIM)
    v = v.reshape(b, nm, CROSS_HEADS, CROSS_HEAD_DIM)
    logits = jnp.einsum('bqhd,bkhd->bhqk', q, k).astype(jnp.float32) * (CROSS_HEAD_DIM ** -0.5)
    p = jax.nn.softmax(logits, axis=-1)
    o = jnp.einsum('bhqk,bkhd->bqhd', p.astype(v.dtype), v).reshape(b, s, D_MODEL)
    return o @ w_o

def setup_inputs(seed: int = 0) -> dict:
    key = jax.random.key(seed)
    ks = iter(jax.random.split(key, 40))
    L = DEPTH

    def dense(shape, fan_in):
        return jax.random.normal(next(ks), shape, jnp.float32) * (fan_in ** -0.5)

    def gain(shape):
        return 1.0 + 0.05 * jax.random.normal(next(ks), shape, jnp.float32)

    def small(shape, scale):
        return scale * jax.random.normal(next(ks), shape, jnp.float32)

    a8 = jax.random.uniform(next(ks), (L, LRU_WIDTH), jnp.float32, 0.9, 0.999)
    a_base = a8 ** (1.0 / LRU_C)
    lru_lambda = jnp.log(a_base) - jnp.log1p(-a_base)
    return {
        "x": jax.random.normal(next(ks), (BATCH, SEQ, D_MODEL), jnp.float32),
        "mem": jax.random.normal(next(ks), (BATCH, N_MEM, D_MODEL), jnp.float32),
        "ffn1_norm": gain((L, D_MODEL)),
        "ffn1_w_in": dense((L, D_MODEL, 2 * D_FF), D_MODEL),
        "ffn1_w_out": dense((L, D_FF, D_MODEL), D_FF),
        "mix_norm": gain((L, D_MODEL)),
        "w_in": dense((L, D_MODEL, MIX_IN), D_MODEL),
        "attn_sinks": small((L, A_HEADS), 0.5),
        "rel_bias": small((L, B_HEADS, 2 * REL_CLIP + 1), 0.1),
        "conv_w": dense((L, CONV_WIDTH, LRU_WIDTH), CONV_WIDTH),
        "conv_b": small((L, LRU_WIDTH), 0.02),
        "rg_a_w": dense((L, LRU_BLOCKS, LRU_BLOCK_W, LRU_BLOCK_W), LRU_BLOCK_W),
        "rg_a_b": small((L, LRU_WIDTH), 0.02),
        "rg_x_w": dense((L, LRU_BLOCKS, LRU_BLOCK_W, LRU_BLOCK_W), LRU_BLOCK_W),
        "rg_x_b": small((L, LRU_WIDTH), 0.02),
        "lru_lambda": lru_lambda,
        "group_norm": gain((L, MIX_WIDTH)),
        "w_out": dense((L, MIX_WIDTH, D_MODEL), MIX_WIDTH),
        "cross_norm": gain((L, D_MODEL)),
        "mem_norm": gain((L, D_MODEL)),
        "w_cq": dense((L, D_MODEL, D_MODEL), D_MODEL),
        "w_ckv": dense((L, D_MODEL, 2 * D_MODEL), D_MODEL),
        "w_co": dense((L, D_MODEL, D_MODEL), D_MODEL),
        "ffn2_norm": gain((L, D_MODEL)),
        "ffn2_w_in": dense((L, D_MODEL, 2 * D_FF), D_MODEL),
        "ffn2_w_out": dense((L, D_FF, D_MODEL), D_FF),
        "final_norm": gain((D_MODEL,)),
    }

def reference(x, mem, ffn1_norm, ffn1_w_in, ffn1_w_out, mix_norm, w_in, attn_sinks, rel_bias,
              conv_w, conv_b, rg_a_w, rg_a_b, rg_x_w, rg_x_b, lru_lambda, group_norm, w_out,
              cross_norm, mem_norm, w_cq, w_ckv, w_co, ffn2_norm, ffn2_w_in, ffn2_w_out, final_norm):
    b, s, _ = x.shape
    cos, sin = rotary_tables(s)
    for l in range(DEPTH):
        x = x + 0.5 * swiglu(rms_norm(x, ffn1_norm[l]), ffn1_w_in[l], ffn1_w_out[l])

        h = rms_norm(x, mix_norm[l])
        qa, ka, va, qb, kb, vb, xr, gate = jnp.split(h @ w_in[l], MIX_SPLITS, axis=-1)
        qa = apply_partial_rope(qa.reshape(b, s, A_HEADS, HEAD_DIM), cos, sin)
        ka = apply_partial_rope(ka.reshape(b, s, A_KV_HEADS, HEAD_DIM), cos, sin)
        va = va.reshape(b, s, A_KV_HEADS, HEAD_DIM)
        y_a = sliding_window_sink_attention(qa, ka, va, attn_sinks[l])
        y_b = chunk_relbias_attention(qb.reshape(b, s, B_HEADS, HEAD_DIM),
                                      kb.reshape(b, s, B_HEADS, HEAD_DIM),
                                      vb.reshape(b, s, B_HEADS, HEAD_DIM), rel_bias[l])
        xr = causal_depthwise_conv(xr, conv_w[l], conv_b[l])
        y_c = jax.nn.gelu(gate) * rg_lru(xr, rg_a_w[l], rg_a_b[l], rg_x_w[l], rg_x_b[l], lru_lambda[l])
        g_a, g_b, g_c = jnp.split(group_norm[l], GROUP_SPLITS)
        y = jnp.concatenate([rms_norm(y_a, g_a), rms_norm(y_b, g_b), rms_norm(y_c, g_c)], axis=-1)
        x = x + y @ w_out[l]

        x = x + cross_attention(rms_norm(x, cross_norm[l]), rms_norm(mem, mem_norm[l]),
                                w_cq[l], w_ckv[l], w_co[l])

        x = x + 0.5 * swiglu(rms_norm(x, ffn2_norm[l]), ffn2_w_in[l], ffn2_w_out[l])
    return rms_norm(x, final_norm)


_drawn_inputs = setup_inputs


def setup_inputs(seed=0):
    import zlib

    import numpy as np

    out = dict(_drawn_inputs(seed))
    spreads = {}
    factors = {'attn_sinks': 8.0,
     'rg_a_b': 8.0,
     'rg_x_b': 8.0,
     'cross_norm': 8.0,
     'mem_norm': 7.587,
     'ffn2_norm': 3.12}
    for name, (base, spread) in spreads.items():
        noise = np.random.default_rng([zlib.crc32(name.encode()), seed]).standard_normal(out[name].shape)
        drawn = base * np.exp(spread * noise) if base else spread * noise
        out[name] = __import__('jax').numpy.asarray(drawn.astype(out[name].dtype))
    for name, factor in factors.items():
        out[name] = (out[name] * factor).astype(out[name].dtype)
    return out
```

```python
from contextlib import ExitStack

import numpy as np

import concourse.bass as bass
from concourse import mybir

F32 = mybir.dt.float32
F32R = mybir.dt.float32r
ALU = mybir.AluOpType
ACT = mybir.ActivationFunctionType
AX_X = mybir.AxisListType.X

P = 128
D = 1024
SEQ = 256
DEPTH = 2
TT = SEQ // P
KD = D // P
CHUNK = 64
HD = 64
A_WIDTH = B_WIDTH = 384
LRU_W = 256
LT = LRU_W // P
A_HEADS = B_HEADS = 6
REL_CLIP = 256
ROT = 16
THETA = 500000.0
CROSS_HEADS = 4
D_FF = 2816
EPS = 1e-6
NEG = -1e30
GELU_CUBE = 0.044715
GELU_SCALE = float(np.sqrt(2.0 / np.pi))

UNIT = 2048
SLOTS = 3
FFN_STEPS = D_FF // 256
FFN_UNITS = 3 * FFN_STEPS
U_FFN1 = 0
U_CK = [33, 34, 44, 45]
U_XR, U_GATE = 35, 36
U_V = 37
U_AQK = [39, 40]
U_BQK = [41, 42, 43]
U_CV = [46, 52]
U_WOUT = 48
U_CQ = 54
U_CO = 58
U_FFN2 = 62
UNITS = U_FFN2 + FFN_UNITS
SLOT_USES = [(UNITS - s + SLOTS - 1) // SLOTS for s in range(SLOTS)]

S_GAIN = {"ffn1": 0, "mix": 8, "group": 16, "cross": 24, "mem": 32, "ffn2": 40}
S_CONVW, S_CONVB, S_BA, S_BX, S_LAM, S_SINK, S_RG = 48, 56, 58, 60, 62, 64, 70
SMALL = S_RG + 4 * P
C_ID, C_FLIP, C_ROT, C_COS, C_SIN, C_MASK = 0, 128, 256, 384, 640, 896
CONSTS = C_MASK + 256

ACC = [0, 1, 2, 3]
GU = [4, 5]
TP = [6, 7]
XB = GU + TP

A_ORDER = [0, 3, 1, 4, 2, 5]

KV_BANK = [0, 1, 1, 0, 0, 1, 0, 1]
N_NORM, N_RESID, N_GU, N_HT, N_KV, N_PROJ, N_HEADS = 5, 8, 4 * FFN_STEPS, 2 * FFN_STEPS, 8, 9, 16
N_DVE = 95
CREDIT = 3


def col(i):
    return A_ORDER[i] if i < A_HEADS else i


def slot_of(pos):
    return pos % SLOTS


def prior_unit(pos):
    if pos >= SLOTS:
        return pos - SLOTS
    last = max(q for q in range(UNITS) if q % SLOTS == pos % SLOTS)
    return last - UNITS


def trunk_kernel(nc, x, mem, stream, small_dram, rel_dram, final_gain, consts_dram, out):
    with ExitStack() as ctx:
        def sb(name, shape, dt=F32):
            return ctx.enter_context(nc.sbuf_tensor(name, shape, dt))

        def sem(name):
            return ctx.enter_context(nc.semaphore(name))

        raw = sb("raw", [P, SLOTS, UNIT])
        w_hi = sb("w_hi", [P, SLOTS, UNIT], F32R)
        w_lo = sb("w_lo", [P, SLOTS, UNIT], F32R)
        resid = sb("resid", [P, TT, D])
        xn = sb("xn", [P, TT, D])
        pair = sb("pair", [P, KD, 2 * SEQ], F32R)
        mem_t = sb("mem_t", [P, KD, SEQ])
        mem_pair = sb("mem_pair", [P, KD, 2 * SEQ], F32R)
        hid_pair = sb("hid_pair", [P, 2, 2 * SEQ], F32R)
        ffn_tmp = sb("ffn_tmp", [P, 1040])
        ck = sb("ck", [P, KD, SEQ])
        cv = sb("cv", [P, TT, D])
        y = sb("y", [P, TT, D])
        probs = sb("probs", [P, 2, 512])
        probs_t = sb("probs_t", [P, 2, 512])
        mix = sb("mix", [P, 4608])
        bias = sb("bias", [P, DEPTH, B_HEADS * 256])
        consts = sb("consts", [P, CONSTS])
        small = sb("small", [P, SMALL])
        sums = sb("sums", [P, 8])
        rstd = sb("rstd", [P, 8])
        expo = sb("expo", [P, 8])
        eps = sb("eps", [P, 8])
        per_width = sb("per_width", [P, 8])
        row_max = sb("row_max", [P, TT, N_HEADS])
        neg_max = sb("neg_max", [P, TT, N_HEADS])
        denom = sb("denom", [P, TT, N_HEADS])
        sink_exp = sb("sink_exp", [P, TT, A_HEADS])
        sp = sb("sp", [P, 32])
        ps = ctx.enter_context(nc.psum_tensor("ps", [P, 8, 512], F32))

        silu = ffn_tmp[:, 0:512].rearrange("p (t n) -> p t n", t=2)
        hid = ffn_tmp[:, 512:1024].rearrange("p (t n) -> p t n", t=2)
        conv_in = ffn_tmp[:, 0:518].rearrange("p (c n) -> p c n", c=LT)
        conv_out = ffn_tmp[:, 518:1030].rearrange("p (c n) -> p c n", c=LT)
        conv_in_flat = ffn_tmp[:, 0:512]
        gate = xn[:, 0, 0:512]
        gelu = xn[:, 0, 512:1024]
        y_lru = xn[:, 1, 0:512].rearrange("p (c n) -> p c n", c=LT)
        lru = cv[:, :, :].rearrange("p t (a n) -> p (t a) n", a=2)
        qk_a_raw = mix[:, 0:1024].rearrange("p (j n) -> p j n", j=4)
        qk_a = mix[:, 1024:2048].rearrange("p (j n) -> p j n", j=4)
        qk_b = mix[:, 2048:3584].rearrange("p (j n) -> p j n", j=6)
        v_ab = mix[:, 3584:4608].rearrange("p (t n) -> p t n", t=TT)
        cq = mix[:, 0:2048].rearrange("p (k n) -> p k n", k=KD)
        hankel = mix[:, 0:3072].rearrange("p (g n) -> p g n", g=DEPTH * B_HEADS)
        ident = consts[:, C_ID:C_ID + P]
        flip = consts[:, C_FLIP:C_FLIP + P]
        rot_t = consts[:, C_ROT:C_ROT + P]
        cos = consts[:, C_COS:C_COS + SEQ]
        sin = consts[:, C_SIN:C_SIN + SEQ]
        window_mask = consts[:, C_MASK:C_MASK + 256]

        def gain(name, k):
            return small[:, S_GAIN[name] + k:S_GAIN[name] + k + 1]

        consts_landed, x_landed, mem_landed, hankel_landed = (
            sem("consts_landed"), sem("x_landed"), sem("mem_landed"), sem("hankel_landed"))
        mem_squares, mem_rstd, mem_scaled, mem_turned, mem_kept = (
            sem("mem_squares"), sem("mem_rstd"), sem("mem_scaled"), sem("mem_turned"), sem("mem_kept"))
        flip_ready, bias_kept, root_consts_ready = sem("flip_ready"), sem("bias_kept"), sem("root_consts_ready")
        raw_landed = [sem(f"raw_landed{s}") for s in range(SLOTS)]
        hi_ready, lo_ready, unit_used = sem("hi_ready"), sem("lo_ready"), sem("unit_used")
        small_landed = sem("small_landed")
        squares_ready, rstd_ready, xn_ready = sem("squares_ready"), sem("rstd_ready"), sem("xn_ready")
        xn_turned, pair_hi_ready, pair_lo_ready = sem("xn_turned"), sem("pair_hi_ready"), sem("pair_lo_ready")
        mem_hi_ready, mem_lo_ready = sem("mem_hi_ready"), sem("mem_lo_ready")
        gate_up_ready, silu_ready, hid_ready = sem("gate_up_ready"), sem("silu_ready"), sem("hid_ready")
        hid_turned, hid_hi_ready, hid_lo_ready = sem("hid_turned"), sem("hid_hi_ready"), sem("hid_lo_ready")
        acc_ready, resid_ready = sem("acc_ready"), sem("resid_ready")
        kv_kept = sem("kv_kept")
        proj_kept, xr_kept = sem("proj_kept"), sem("xr_kept")
        conv_ready, gates_ready, gates_exp_ready = sem("conv_ready"), sem("gates_ready"), sem("gates_exp_ready")
        sig_ready, decay_ready, gain2_ready, root_ready = (
            sem("sig_ready"), sem("decay_ready"), sem("gain2_ready"), sem("root_ready"))
        cube_ready, gelu_tanh_ready, y_lru_ready, y_lru_turned = (
            sem("cube_ready"), sem("gelu_tanh_ready"), sem("y_lru_ready"), sem("y_lru_turned"))
        lam_ready, lam_exp_ready, decay_scale_ready = sem("lam_ready"), sem("lam_exp_ready"), sem("decay_scale_ready")
        rope_turned, rope_ready = sem("rope_turned"), sem("rope_ready")
        scores_ready, max_ready, probs_ready = sem("scores_ready"), sem("max_ready"), sem("probs_ready")
        probs_turned, probs_t_kept = sem("probs_turned"), sem("probs_t_kept")
        y_kept, cq_kept = sem("y_kept"), sem("cq_kept")
        y_ready, sink_ready, sink_exp_ready = sem("y_ready"), sem("sink_ready"), sem("sink_exp_ready")
        probs_scaled, o_ready, o_hi_ready, o_lo_ready = (
            sem("probs_scaled"), sem("o_ready"), sem("o_hi_ready"), sem("o_lo_ready"))
        dve_step, pool_step, act_step = sem("dve_step"), sem("pool_step"), sem("act_step")
        last_squares, last_rstd, result_ready, gain_landed, stored = (
            sem("last_squares"), sem("last_rstd"), sem("result_ready"), sem("gain_landed"), sem("stored"))

        block = ctx.enter_context(nc.Block())

        @block.sync
        def _(sp_eng):
            sp_eng.dma_start(xn[:, :, :], mem.rearrange("b (t p) d -> p (b t) d", p=P)).then_inc(mem_landed, 16)
            sp_eng.dma_start(consts[:, :], consts_dram).then_inc(consts_landed, 16)
            sp_eng.dma_start(resid[:, :, :], x.rearrange("b (t p) d -> p (b t) d", p=P)).then_inc(x_landed, 16)
            sp_eng.dma_start(hankel, bass.AP(rel_dram.tensor, 1, [[1, P], [2 * REL_CLIP + 1, DEPTH * B_HEADS], [1, 256]]))\
                  .then_inc(hankel_landed, 16)

            def load_unit(layer, pos, turn=0):
                s = slot_of(pos)
                sp_eng.wait_ge(lo_ready, layer * UNITS + turn * SLOTS + prior_unit(pos) + 1 + CREDIT)
                sp_eng.dma_start(
                    raw[:, s, :],
                    stream[bass.ds(layer * UNITS + turn * SLOTS + pos, 1), :, :].rearrange("a p n -> p (a n)"),
                ).then_inc(raw_landed[s], 16)

            with sp_eng.Fori(0, DEPTH) as layer:
                for pos in range(SLOTS):
                    load_unit(layer, pos)
                with sp_eng.Fori(0, UNITS // SLOTS - 1) as turn:
                    for s in range(SLOTS):
                        load_unit(layer, SLOTS + s, turn)
                for pos in range(UNITS // SLOTS * SLOTS, UNITS):
                    load_unit(layer, pos)
            sp_eng.wait_ge(xn_ready, (DEPTH - 1) * TT * N_NORM + 3 * TT)
            sp_eng.dma_start(y[:, 0, :], final_gain.partition_broadcast(P)).then_inc(gain_landed, 16)
            for t in range(TT):
                sp_eng.wait_ge(result_ready, t + 1)
                sp_eng.dma_start(out[0, t * P:(t + 1) * P, :], xn[:, t, :]).then_inc(stored, 16)
            sp_eng.wait_ge(stored, 16 * TT)

        @block.gpsimd
        def _(pool):
            pool.memset(expo[:, :], -0.5).then_inc(root_consts_ready, 1)
            pool.memset(eps[:, :], EPS).then_inc(root_consts_ready, 1)
            pool.memset(per_width[:, 0:2], 1.0 / D).then_inc(root_consts_ready, 1)
            pool.memset(per_width[:, 2:6], 1.0 / A_WIDTH).then_inc(root_consts_ready, 1)
            pool.memset(per_width[:, 6:8], 1.0 / LRU_W).then_inc(root_consts_ready, 1)
            pool.wait_ge(root_consts_ready, 5)

            def roots(step, groups, signal):
                n, at = (6, 2) if groups else (2, 0)
                cols = rstd[:, 0:n]
                pool.tensor_tensor(cols, sums[:, 0:n], per_width[:, at:at + n], ALU.mult).then_inc(pool_step, 1)
                pool.wait_ge(pool_step, 2 * step + 1)
                pool.tensor_tensor(cols, cols, eps[:, 0:n], ALU.add).then_inc(pool_step, 1)
                pool.wait_ge(pool_step, 2 * step + 2)
                pool.tensor_tensor(cols, cols, expo[:, 0:n], ALU.pow).then_inc(signal, 1)

            pool.wait_ge(mem_squares, 1)
            roots(0, False, mem_rstd)
            with pool.Fori(0, DEPTH) as layer:
                for n in range(N_NORM):
                    pool.wait_ge(squares_ready, layer * N_NORM + n + 1)
                    roots(layer * N_NORM + n + 1, n == 2, rstd_ready)
            pool.wait_ge(last_squares, 1)
            roots(DEPTH * N_NORM + 1, False, last_rstd)

        @block.scalar
        def _(act):
            def after_unit(layer, pos, turn=0):
                act.wait_ge(unit_used, layer * UNITS + turn * SLOTS + pos + 1 + CREDIT)

            def split_hi(layer, pos, turn=0):
                s = slot_of(pos)
                act.wait_ge(raw_landed[s], (layer * SLOT_USES[s] + turn + pos // SLOTS + 1) * 16)
                act.wait_ge(unit_used, layer * UNITS + turn * SLOTS + prior_unit(pos) + 1 + CREDIT)
                nc.scalar.activation(w_hi[:, s, :], raw[:, s, :], ACT.Copy).then_inc(hi_ready, 1)

            def turn_pairs(layer, n, name):
                for kp in range(KD // 2):
                    act.wait_ge(xn_turned, layer * 4 * N_NORM + 4 * n + kp + 1)
                    for k in (2 * kp, 2 * kp + 1):
                        ins = nc.scalar.activation(pair[:, k, 0:SEQ], ps[:, XB[kp], (k % 2) * SEQ:(k % 2 + 1) * SEQ],
                                                   ACT.Copy, scale=gain(name, k))
                    ins.then_inc(pair_hi_ready, 1)

            def norm_squares(layer, n, use):
                for t in range(TT):
                    act.wait_ge(resid_ready, layer * N_RESID + 2 * use + t + 1)
                    ins = nc.scalar.activation(xn[:, t, :], resid[:, t, :], ACT.Square, accum_out=sums[:, t:t + 1])
                ins.then_inc(squares_ready, 1)

            def ffn_step(layer, f, it, last_unit, turn=0):
                for t in range(TT):
                    if t == 0:
                        act.wait_ge(gate_up_ready, layer * 2 * FFN_STEPS + f * FFN_STEPS + it + 1)
                    else:
                        after_unit(layer, last_unit, turn)
                    nc.scalar.activation(silu[:, t, :], ps[:, GU[t], 0:256], ACT.Silu).then_inc(silu_ready, 1)

            def hid_hi(layer, f, it):
                act.wait_ge(hid_turned, layer * N_HT + f * FFN_STEPS + it + 1)
                nc.scalar.activation(hid_pair[:, :, 0:SEQ], ps[:, TP[0], :].rearrange("p (k n) -> p k n", k=2),
                                     ACT.Copy).then_inc(hid_hi_ready, 1)

            def ffn(layer, f, first, after_first=None):
                split_hi(layer, first + 2)
                ffn_step(layer, f, 0, first + 1)
                split_hi(layer, first + 3)
                hid_hi(layer, f, 0)
                if after_first:
                    after_first()
                with act.Fori(0, FFN_STEPS - 2) as turn:
                    split_hi(layer, first + 4, turn)
                    ffn_step(layer, f, turn + 1, first + 3, turn)
                    split_hi(layer, first + 5, turn)
                    split_hi(layer, first + 6, turn)
                    hid_hi(layer, f, turn + 1)
                last = FFN_STEPS - 1
                split_hi(layer, first + 3 * last + 1)
                ffn_step(layer, f, last, first + 3 * last)
                split_hi(layer, first + 3 * last + 2)
                if first + 3 * last + 3 < UNITS:
                    split_hi(layer, first + 3 * last + 3)
                hid_hi(layer, f, last)

            def copy(out_ap, in_ap, signal):
                nc.scalar.activation(out_ap, in_ap, ACT.Copy).then_inc(signal, 1)

            def keep_kv(layer, i):
                order = [("k", 0), ("k", 1), ("k", 2), ("k", 3), ("v", 0), ("v", 1), ("v", 2), ("v", 3)]
                kind, j = order[i]
                after_unit(layer, U_CK[j] if kind == "k" else U_CV[j // 2] + 1)
                if kind == "k":
                    copy(ck[:, 2 * j:2 * j + 2, :], ps[:, ACC[2 + KV_BANK[i]], :].rearrange("p (c n) -> p c n", c=2), kv_kept)
                else:
                    t, half = j % 2, j // 2
                    copy(cv[:, t, half * 512:(half + 1) * 512], ps[:, ACC[2 + KV_BANK[i]], :], kv_kept)

            def head_probs(layer, i):
                act.wait_ge(max_ready, layer * N_HEADS + i + 1)
                b = i % 2
                if i < 12:
                    for t, lo_, hi_ in ((0, 0, 128), (1, 128, 384)):
                        ins = nc.scalar.activation(probs[:, b, lo_:hi_], probs[:, b, lo_:hi_], ACT.Exp,
                                                   bias=neg_max[:, t, col(i):col(i) + 1],
                                                   accum_out=denom[:, t, col(i):col(i) + 1])
                else:
                    act.wait_ge(probs_turned, layer * N_HEADS + i - 1)
                    for t in range(TT):
                        ins = nc.scalar.activation(probs[:, b, t * 256:(t + 1) * 256],
                                                   ps[:, GU[b], t * 256:(t + 1) * 256], ACT.Exp, scale=1.0 / 16,
                                                   bias=neg_max[:, t, col(i):col(i) + 1],
                                                   accum_out=denom[:, t, col(i):col(i) + 1])
                ins.then_inc(probs_ready, 1)

            def keep_probs_t(layer, i):
                n = 384 if i < 12 else 512
                act.wait_ge(probs_turned, layer * N_HEADS + i + 1)
                copy(probs_t[:, i % 2, 0:n], ps[:, TP[i % 2], 0:n], probs_t_kept)

            def o_hi(layer, h):
                act.wait_ge(o_ready, layer * CROSS_HEADS + h + 1)
                nc.scalar.activation(pair[:, 2 * h:2 * h + 2, 0:SEQ], ps[:, ACC[h], :].rearrange("p (c n) -> p c n", c=2),
                                     ACT.Copy).then_inc(o_hi_ready, 1)

            act.wait_ge(mem_landed, 16)
            for t in range(TT):
                ins = nc.scalar.activation(ps[:, 2 * t:2 * t + 2, :], xn[:, t, :].rearrange("p (a n) -> p a n", a=2),
                                           ACT.Square, accum_out=sums[:, t:t + 1])
            ins.then_inc(mem_squares, 1)
            for kp in range(KD // 2):
                act.wait_ge(mem_turned, kp + 1)
                copy(mem_t[:, 2 * kp:2 * kp + 2, :], ps[:, XB[kp], :].rearrange("p (c n) -> p c n", c=2), mem_kept)

            with act.Fori(0, DEPTH) as layer:
                split_hi(layer, 0)
                norm_squares(layer, 0, 0)
                act.dma_start(small[:, :], small_dram[bass.ds(layer, 1), :, :].rearrange("a p n -> p (a n)"))\
                   .then_inc(small_landed, 16)
                split_hi(layer, 1)
                act.wait_ge(small_landed, (layer + 1) * 16)
                turn_pairs(layer, 0, "ffn1")

                def mem_times_gain():
                    for k in range(KD):
                        ins = nc.scalar.activation(mem_pair[:, k, 0:SEQ], mem_t[:, k, :], ACT.Copy, scale=gain("mem", k))
                    ins.then_inc(mem_hi_ready, 1)
                    act.wait_ge(lam_ready, layer + 1)
                    nc.scalar.activation(sp[:, 4:6], sp[:, 2:4], ACT.Exp).then_inc(lam_exp_ready, 1)

                act.wait_ge(mem_kept, KD // 2)
                ffn(layer, 0, U_FFN1, mem_times_gain)
                split_hi(layer, 34)
                norm_squares(layer, 1, 1)
                keep_kv(layer, 0)
                split_hi(layer, 35)
                keep_kv(layer, 1)
                split_hi(layer, 36)
                turn_pairs(layer, 1, "mix")

                def keep_proj(i, out_ap, bank, shape=None):
                    after_unit(layer, (U_XR, U_GATE, U_V + 1, U_V + 1, *U_AQK, *U_BQK)[i])
                    src = ps[:, bank, :]
                    copy(out_ap, src.rearrange("p (c n) -> p c n", c=2) if shape else src, proj_kept)

                split_hi(layer, 37)
                keep_proj(1, gate, ACC[1])
                split_hi(layer, 38)
                split_hi(layer, 39)
                keep_proj(2, v_ab[:, 0, :], GU[0])
                keep_proj(3, v_ab[:, 1, :], GU[1])
                split_hi(layer, 40)
                act.wait_ge(cube_ready, layer + 1)
                nc.scalar.activation(gelu, gelu, ACT.Tanh, scale=GELU_SCALE).then_inc(gelu_tanh_ready, 1)
                keep_proj(4, qk_a_raw[:, 0:2, :], ACC[2], 2)
                split_hi(layer, 41)
                keep_proj(5, qk_a_raw[:, 2:4, :], ACC[3], 2)
                split_hi(layer, 42)
                split_hi(layer, 43)
                act.wait_ge(gates_ready, layer + 1)
                act.wait_ge(decay_scale_ready, layer + 1)
                for g in range(2):
                    for c in range(LT):
                        ins = nc.scalar.activation(lru[:, g, c * SEQ:(c + 1) * SEQ], ps[:, ACC[g], c * SEQ:(c + 1) * SEQ],
                                                   ACT.Exp, scale=-1.0, bias=sp[:, 20 + 2 * g + c:21 + 2 * g + c])
                ins.then_inc(gates_exp_ready, 1)

                def lru_decay():
                    act.wait_ge(sig_ready, layer + 1)
                    for c in range(LT):
                        for j, func in ((2, ACT.Exp), (3, ACT.Tanh)):
                            ins = nc.scalar.activation(lru[:, j, c * SEQ:(c + 1) * SEQ], lru[:, 0, c * SEQ:(c + 1) * SEQ],
                                                       func, scale=sp[:, 18 + c:19 + c])
                    ins.then_inc(decay_ready, 1)

                def lru_root():
                    act.wait_ge(gain2_ready, layer + 1)
                    nc.scalar.activation(lru[:, 3, :], lru[:, 3, :], ACT.Sqrt, scale=-1.0).then_inc(root_ready, 1)

                for i in range(12 + 1):
                    if i < 12:
                        head_probs(layer, i)
                    if i >= 1:
                        keep_probs_t(layer, i - 1)
                    if i == 0:
                        keep_proj(6, qk_b[:, 0:2, :], ACC[2], 2)
                        split_hi(layer, 44)
                        lru_decay()
                    if i == 2:
                        keep_proj(7, qk_b[:, 2:4, :], ACC[3], 2)
                        split_hi(layer, 45)
                        lru_root()
                    if i == 4:
                        keep_proj(8, qk_b[:, 4:6, :], ACC[2], 2)
                        split_hi(layer, 46)
                    if i == 6:
                        act.wait_ge(sink_ready, layer + 1)
                        nc.scalar.activation(sink_exp[:, :, :], sink_exp[:, :, :], ACT.Exp).then_inc(sink_exp_ready, 1)
                    if i == 7:
                        keep_kv(layer, 2)
                        split_hi(layer, 47)
                    if i == 9:
                        keep_kv(layer, 3)
                        split_hi(layer, 48)

                act.wait_ge(y_kept, 3 * layer + 3)
                for g, (lo_, hi_) in enumerate(((0, 384), (384, 768), (768, 1024))):
                    for t in range(TT):
                        ins = nc.scalar.activation(xn[:, t, lo_:hi_], y[:, t, lo_:hi_], ACT.Square,
                                                   accum_out=sums[:, 2 * g + t:2 * g + t + 1])
                ins.then_inc(squares_ready, 1)
                keep_kv(layer, 4)
                keep_kv(layer, 5)
                split_hi(layer, 49)
                split_hi(layer, 50)
                turn_pairs(layer, 2, "group")
                split_hi(layer, 51)
                split_hi(layer, 52)
                split_hi(layer, 53)
                norm_squares(layer, 3, 2)
                keep_kv(layer, 6)
                keep_kv(layer, 7)
                split_hi(layer, 54)
                split_hi(layer, 55)
                turn_pairs(layer, 3, "cross")
                for u in range(4):
                    split_hi(layer, 56 + u)
                    after_unit(layer, U_CQ + u)
                    copy(cq[:, 2 * u:2 * u + 2, :], ps[:, ACC[u], :].rearrange("p (c n) -> p c n", c=2), cq_kept)
                split_hi(layer, 60)
                for i in range(12, 16):
                    head_probs(layer, i)
                    if i >= 13:
                        keep_probs_t(layer, i - 1)
                    if i >= 14:
                        o_hi(layer, i - 14)
                keep_probs_t(layer, 15)
                o_hi(layer, 2)
                o_hi(layer, 3)
                split_hi(layer, 61)
                split_hi(layer, 62)
                split_hi(layer, 63)
                norm_squares(layer, 4, 3)
                turn_pairs(layer, 4, "ffn2")
                ffn(layer, 1, U_FFN2)

            for t in range(TT):
                act.wait_ge(resid_ready, DEPTH * N_RESID + t + 1)
                ins = nc.scalar.activation(xn[:, t, :], resid[:, t, :], ACT.Square, accum_out=sums[:, t:t + 1])
            ins.then_inc(last_squares, 1)

        @block.vector
        def _(dve):
            steps = [0]

            def step(ins):
                ins.then_inc(dve_step, 1)
                steps[0] += 1

            def after_step(layer):
                dve.wait_ge(dve_step, layer * N_DVE + steps[0] + 1)

            def after_unit(layer, pos, turn=0):
                dve.wait_ge(unit_used, layer * UNITS + turn * SLOTS + pos + 1 + CREDIT)

            def split_lo(layer, pos, turn=0):
                s = slot_of(pos)
                dve.wait_ge(hi_ready, layer * UNITS + turn * SLOTS + pos + 1)
                nc.vector.tensor_tensor(w_lo[:, s, :], raw[:, s, :], w_hi[:, s, :].bitcast(F32),
                                        ALU.subtract).then_inc(lo_ready, 1)

            def scale_rows(layer, n):
                dve.wait_ge(rstd_ready, layer * N_NORM + n + 1)
                for t in range(TT):
                    if n == 2:
                        for g, (lo_, hi_) in enumerate(((0, 384), (384, 768), (768, 1024))):
                            ins = nc.vector.tensor_scalar(xn[:, t, lo_:hi_], y[:, t, lo_:hi_],
                                                          rstd[:, 2 * g + t:2 * g + t + 1], None, ALU.mult)
                    else:
                        ins = nc.vector.tensor_scalar(xn[:, t, :], resid[:, t, :], rstd[:, t:t + 1], None, ALU.mult)
                    ins.then_inc(xn_ready, 1)

            def turn_pairs(layer, n, name):
                for kp in range(KD // 2):
                    dve.wait_ge(pair_hi_ready, layer * 4 * N_NORM + 4 * n + kp + 1)
                    for k in (2 * kp, 2 * kp + 1):
                        ins = nc.vector.scalar_tensor_tensor(
                            out=pair[:, k, SEQ:2 * SEQ], in0=ps[:, XB[kp], (k % 2) * SEQ:(k % 2 + 1) * SEQ],
                            scalar=gain(name, k), in1=pair[:, k, 0:SEQ].bitcast(F32), op0=ALU.mult, op1=ALU.subtract)
                    ins.then_inc(pair_lo_ready, 1)

            def add_residual(layer, use, scale):
                for t in range(TT):
                    if t == 0:
                        dve.wait_ge(acc_ready, layer * (N_RESID // TT) + use + 1)
                    else:
                        after_unit(layer, (U_FFN1 + FFN_UNITS - 1, U_WOUT + 3, U_CO + 3, U_FFN2 + FFN_UNITS - 1)[use])
                    for c in range(2):
                        cols = slice(c * 512, (c + 1) * 512)
                        ins = nc.vector.scalar_tensor_tensor(out=resid[:, t, cols], in0=ps[:, ACC[2 * t + c], :],
                                                             scalar=scale, in1=resid[:, t, cols],
                                                             op0=ALU.mult, op1=ALU.add)
                    ins.then_inc(resid_ready, 1)

            def ffn_step(layer, f, it):
                for t in range(TT):
                    dve.wait_ge(silu_ready, layer * N_GU + (f * FFN_STEPS + it) * TT + t + 1)
                    nc.vector.tensor_tensor(hid[:, t, :], silu[:, t, :], ps[:, GU[t], 256:512],
                                            ALU.mult).then_inc(hid_ready, 1)

            def hid_lo(layer, f, it):
                dve.wait_ge(hid_hi_ready, layer * N_HT + f * FFN_STEPS + it + 1)
                nc.vector.tensor_tensor(hid_pair[:, :, SEQ:2 * SEQ], ps[:, TP[0], :].rearrange("p (k n) -> p k n", k=2),
                                        hid_pair[:, :, 0:SEQ].bitcast(F32), ALU.subtract).then_inc(hid_lo_ready, 1)

            def ffn(layer, f, first, after_first=None):
                split_lo(layer, first + 2)
                ffn_step(layer, f, 0)
                split_lo(layer, first + 3)
                hid_lo(layer, f, 0)
                if after_first:
                    after_first()
                with dve.Fori(0, FFN_STEPS - 2) as turn:
                    split_lo(layer, first + 4, turn)
                    ffn_step(layer, f, turn + 1)
                    split_lo(layer, first + 5, turn)
                    split_lo(layer, first + 6, turn)
                    hid_lo(layer, f, turn + 1)
                last = FFN_STEPS - 1
                split_lo(layer, first + 3 * last + 1)
                ffn_step(layer, f, last)
                split_lo(layer, first + 3 * last + 2)
                if first + 3 * last + 3 < UNITS:
                    split_lo(layer, first + 3 * last + 3)
                hid_lo(layer, f, last)

            def decay_scale(layer):
                lam = small[:, S_LAM:S_LAM + LT]
                step(nc.vector.tensor_scalar(sp[:, 0:2], lam, -1.0, None, ALU.mult))
                step(nc.vector.tensor_scalar(sp[:, 20:24], small[:, S_BA:S_BA + 4], -1.0, None, ALU.mult))
                after_step(layer)
                nc.vector.tensor_tensor(sp[:, 2:4], sp[:, 0:2], lam, ALU.min).then_inc(lam_ready, 1)
                dve.wait_ge(lam_exp_ready, layer + 1)
                step(nc.vector.tensor_scalar(sp[:, 6:8], sp[:, 4:6], 2.0, None, ALU.add))
                after_step(layer)
                step(nc.vector.reciprocal(sp[:, 8:10], sp[:, 6:8]))
                after_step(layer)
                step(nc.vector.tensor_tensor(sp[:, 10:12], sp[:, 4:6], sp[:, 8:10], ALU.mult))
                after_step(layer)
                step(nc.vector.tensor_tensor(sp[:, 12:14], sp[:, 10:12], sp[:, 10:12], ALU.mult))
                after_step(layer)
                step(nc.vector.tensor_scalar(sp[:, 14:16], sp[:, 12:14], 1.0 / 17, None, ALU.mult))
                for odd in (15, 13, 11, 9, 7, 5, 3):
                    after_step(layer)
                    step(nc.vector.scalar_tensor_tensor(out=sp[:, 14:16], in0=sp[:, 14:16], scalar=1.0 / odd,
                                                        in1=sp[:, 12:14], op0=ALU.add, op1=ALU.mult))
                after_step(layer)
                step(nc.vector.scalar_tensor_tensor(out=sp[:, 14:16], in0=sp[:, 14:16], scalar=1.0,
                                                    in1=sp[:, 10:12], op0=ALU.add, op1=ALU.mult))
                step(nc.vector.tensor_scalar(sp[:, 16:18], sp[:, 0:2], 0.0, None, ALU.max))
                after_step(layer)
                step(nc.vector.scalar_tensor_tensor(out=sp[:, 14:16], in0=sp[:, 14:16], scalar=2.0,
                                                    in1=sp[:, 16:18], op0=ALU.mult, op1=ALU.add))
                after_step(layer)
                nc.vector.tensor_scalar(sp[:, 18:20], sp[:, 14:16], -8.0, None, ALU.mult).then_inc(decay_scale_ready, 1)

            def head_logits(layer, i):
                b = i % 2
                if i < A_HEADS:
                    table = window_mask
                else:
                    table = bias[:, bass.ds(layer, 1), (i - 6) * 256:(i - 5) * 256].rearrange("p a n -> p (a n)")
                dve.wait_ge(scores_ready, layer * N_HEADS + i + 1)
                step(nc.vector.scalar_tensor_tensor(out=probs[:, b, 0:128], in0=ps[:, GU[b], 0:128], scalar=HD ** -0.5,
                                                    in1=table[:, 128:256], op0=ALU.mult, op1=ALU.add))
                step(nc.vector.scalar_tensor_tensor(out=probs[:, b, 128:384], in0=ps[:, GU[b], 128:384], scalar=HD ** -0.5,
                                                    in1=table, op0=ALU.mult, op1=ALU.add))
                after_step(layer)
                for t, lo_, hi_ in ((0, 0, 128), (1, 128, 384)):
                    step(nc.vector.reduce_max(row_max[:, t, col(i):col(i) + 1], probs[:, b, lo_:hi_], AX_X))
                after_step(layer)
                out_, in_ = neg_max[:, :, col(i)], row_max[:, :, col(i)]
                if i < A_HEADS:
                    sink = small[:, S_SINK + col(i):S_SINK + col(i) + 1]
                    nc.vector.tensor_scalar(out_, in_, sink, -1.0, ALU.max, ALU.mult).then_inc(max_ready, 1)
                else:
                    nc.vector.tensor_scalar(out_, in_, -1.0, None, ALU.mult).then_inc(max_ready, 1)

            def keep_y(layer, g):
                dve.wait_ge(y_ready, 2 * layer + g + 1)
                for t in range(TT):
                    scale = denom[:, t, 6 * g:6 * g + 6].unsqueeze(2).to_broadcast([P, 6, HD])
                    ins = nc.vector.tensor_tensor(
                        y[:, t, g * 384:(g + 1) * 384].rearrange("p (h d) -> p h d", h=6),
                        ps[:, ACC[t], 0:384].rearrange("p (h d) -> p h d", h=6), scale, ALU.mult)
                ins.then_inc(y_kept, 1)

            dve.sem_inc(lo_ready, CREDIT)
            dve.wait_ge(x_landed, 16)
            dve.sem_inc(resid_ready, TT)
            dve.wait_ge(mem_rstd, 1)
            for t in range(TT):
                nc.vector.tensor_scalar(xn[:, t, :], xn[:, t, :], rstd[:, t:t + 1], None, ALU.mult).then_inc(mem_scaled, 1)
            bias_flat = bias[:, :, :].rearrange("p l n -> p (l n)")
            for j in range(DEPTH * B_HEADS // 2):
                dve.wait_ge(flip_ready, j + 1)
                nc.vector.tensor_copy(bias_flat[:, j * 512:(j + 1) * 512], ps[:, ACC[j % 4], :]).then_inc(bias_kept, 1)
            dve.wait_ge(bias_kept, DEPTH * B_HEADS // 2)
            nc.vector.memset(bias[0:64, :, :].rearrange("p l (h n) -> p (l h) n", n=256)[:, :, 192:256], NEG)\
                     .then_inc(dve_step, 1)

            with dve.Fori(0, DEPTH) as layer:
                split_lo(layer, 0)
                scale_rows(layer, 0)
                split_lo(layer, 1)
                turn_pairs(layer, 0, "ffn1")

                def mem_times_gain():
                    dve.wait_ge(mem_hi_ready, layer + 1)
                    for k in range(KD):
                        ins = nc.vector.scalar_tensor_tensor(
                            out=mem_pair[:, k, SEQ:2 * SEQ], in0=mem_t[:, k, :], scalar=gain("mem", k),
                            in1=mem_pair[:, k, 0:SEQ].bitcast(F32), op0=ALU.mult, op1=ALU.subtract)
                    ins.then_inc(mem_lo_ready, 1)
                    decay_scale(layer)

                ffn(layer, 0, U_FFN1, mem_times_gain)
                add_residual(layer, 0, 0.5)
                split_lo(layer, 34)
                scale_rows(layer, 1)
                split_lo(layer, 35)
                split_lo(layer, 36)
                turn_pairs(layer, 1, "mix")
                split_lo(layer, 37)

                step(nc.vector.memset(conv_in[:, :, 0:3], 0.0))
                after_unit(layer, U_XR)
                nc.vector.tensor_copy(conv_in[:, :, 3:3 + SEQ], ps[:, ACC[0], :].rearrange("p (c n) -> p c n", c=2))\
                         .then_inc(xr_kept, 1)
                after_step(layer)
                dve.wait_ge(xr_kept, layer + 1)
                for j in range(4):
                    for c in range(LT):
                        w = small[:, S_CONVW + 2 * j + c:S_CONVW + 2 * j + c + 1]
                        if j == 0:
                            step(nc.vector.tensor_scalar(conv_out[:, c, :], conv_in[:, c, 0:SEQ], w,
                                                         small[:, S_CONVB + c:S_CONVB + c + 1], ALU.mult, ALU.add))
                            continue
                        ins = nc.vector.scalar_tensor_tensor(out=conv_out[:, c, :], in0=conv_in[:, c, j:j + SEQ], scalar=w,
                                                             in1=conv_out[:, c, :], op0=ALU.mult, op1=ALU.add)
                        if j < 3 or c == 0:
                            step(ins)
                        else:
                            ins.then_inc(conv_ready, 1)
                    if j < 3:
                        after_step(layer)
                split_lo(layer, 38)
                split_lo(layer, 39)
                dve.wait_ge(proj_kept, layer * (N_PROJ - 1) + 1)
                step(nc.vector.tensor_tensor(gelu, gate, gate, ALU.mult))
                after_step(layer)
                step(nc.vector.tensor_scalar(gelu, gelu, GELU_CUBE, 1.0, ALU.mult, ALU.add))
                after_step(layer)
                nc.vector.tensor_tensor(gelu, gelu, gate, ALU.mult).then_inc(cube_ready, 1)
                split_lo(layer, 40)
                split_lo(layer, 41)
                dve.wait_ge(proj_kept, layer * (N_PROJ - 1) + 5)
                over4 = lambda a: a.unsqueeze(1).to_broadcast([P, 4, SEQ])
                step(nc.vector.tensor_tensor(qk_a[:, :, :], qk_a_raw[:, :, :], over4(cos), ALU.mult))
                split_lo(layer, 42)
                dve.wait_ge(rope_turned, layer + 1)
                after_step(layer)
                step(nc.vector.tensor_tensor(qk_a_raw[:, :, :], ps[:, TP[0]:TP[1] + 1, :].rearrange("p b (c n) -> p (b c) n", c=2),
                                             over4(sin), ALU.mult))
                after_step(layer)
                nc.vector.tensor_tensor(qk_a[:, :, :], qk_a[:, :, :], qk_a_raw[:, :, :], ALU.add).then_inc(rope_ready, 1)
                split_lo(layer, 43)

                def lru_sigmoids():
                    dve.wait_ge(gates_exp_ready, layer + 1)
                    step(nc.vector.tensor_scalar(lru[:, 0:2, :], lru[:, 0:2, :], 1.0, None, ALU.add))
                    after_step(layer)
                    nc.vector.reciprocal(lru[:, 0:2, :], lru[:, 0:2, :]).then_inc(sig_ready, 1)

                def lru_input_gain():
                    dve.wait_ge(decay_ready, layer + 1)
                    m = lru[:, 3, :]
                    square = conv_in_flat
                    step(nc.vector.tensor_tensor(square, lru[:, 2, :], lru[:, 2, :], ALU.mult))
                    after_step(layer)
                    nc.vector.scalar_tensor_tensor(out=m, in0=square, scalar=1.0, in1=m, op0=ALU.add,
                                                   op1=ALU.mult).then_inc(gain2_ready, 1)
                    dve.wait_ge(sig_ready, layer + 1)
                    step(nc.vector.tensor_tensor(lru[:, 1, :], lru[:, 1, :],
                                                 conv_out[:, :, :].rearrange("p c n -> p (c n)"), ALU.mult))
                    dve.wait_ge(gelu_tanh_ready, layer + 1)
                    step(nc.vector.scalar_tensor_tensor(out=gelu, in0=gelu, scalar=1.0, in1=gate, op0=ALU.add, op1=ALU.mult))

                def lru_scan():
                    dve.wait_ge(root_ready, layer + 1)
                    after_step(layer)
                    step(nc.vector.tensor_tensor(lru[:, 1, :], lru[:, 1, :], lru[:, 3, :], ALU.mult))
                    after_step(layer)
                    for c in range(LT):
                        cols = slice(c * SEQ, (c + 1) * SEQ)
                        step(nc.vector.tensor_tensor_scan(lru[:, 0, cols], lru[:, 2, cols], lru[:, 1, cols], 0.0,
                                                          ALU.mult, ALU.add))
                    after_step(layer)
                    nc.vector.scalar_tensor_tensor(out=xn[:, 1, 0:512], in0=gelu, scalar=0.5, in1=lru[:, 0, :],
                                                   op0=ALU.mult, op1=ALU.mult).then_inc(y_lru_ready, 1)

                for i in range(12 + 1):
                    if i < 12:
                        if i >= 2:
                            dve.wait_ge(probs_turned, layer * N_HEADS + i - 1)
                        head_logits(layer, i)
                    if i == 0:
                        lru_sigmoids()
                        split_lo(layer, 44)
                    if i == 1:
                        lru_input_gain()
                    if i == 2:
                        split_lo(layer, 45)
                    if i == 3:
                        lru_scan()
                    if i == 4:
                        split_lo(layer, 46)
                    if i == 5:
                        dve.wait_ge(max_ready, layer * N_HEADS + 6)
                        for t in range(TT):
                            ins = nc.vector.tensor_tensor(sink_exp[:, t, :], neg_max[:, t, 0:6],
                                                          small[:, S_SINK:S_SINK + 6], ALU.add)
                        ins.then_inc(sink_ready, 1)
                    if i == 7:
                        dve.wait_ge(sink_exp_ready, layer + 1)
                        step(nc.vector.tensor_tensor(denom[:, :, 0:6], denom[:, :, 0:6], sink_exp[:, :, :], ALU.add))
                        after_step(layer)
                        step(nc.vector.reciprocal(denom[:, :, 0:6], denom[:, :, 0:6]))
                        after_step(layer)
                        keep_y(layer, 0)
                        split_lo(layer, 47)
                    if i == 9:
                        split_lo(layer, 48)
                dve.wait_ge(probs_ready, layer * N_HEADS + 12)
                step(nc.vector.reciprocal(denom[:, :, 6:12], denom[:, :, 6:12]))
                dve.wait_ge(y_lru_turned, layer + 1)
                nc.vector.tensor_copy(y[:, :, 768:1024], ps[:, ACC[3], :].rearrange("p (t n) -> p t n", t=2)).then_inc(y_kept, 1)
                after_step(layer)
                keep_y(layer, 1)

                scale_rows(layer, 2)
                split_lo(layer, 49)
                split_lo(layer, 50)
                turn_pairs(layer, 2, "group")
                split_lo(layer, 51)
                split_lo(layer, 52)
                split_lo(layer, 53)
                add_residual(layer, 1, 1.0)
                scale_rows(layer, 3)
                split_lo(layer, 54)
                split_lo(layer, 55)
                turn_pairs(layer, 3, "cross")
                for u in range(5):
                    split_lo(layer, 56 + u)

                def head_max(i):
                    dve.wait_ge(scores_ready, layer * N_HEADS + i + 1)
                    step(nc.vector.reduce_max(row_max[:, :, i], ps[:, GU[i % 2], :].rearrange("p (t n) -> p t n", t=2), AX_X))
                    after_step(layer)
                    nc.vector.tensor_scalar(neg_max[:, :, i], row_max[:, :, i], -1.0 / 16, None, ALU.mult).then_inc(max_ready, 1)

                def scale_probs(i):
                    dve.wait_ge(probs_ready, layer * N_HEADS + i + 1)
                    step(nc.vector.reciprocal(denom[:, :, i], denom[:, :, i]))
                    after_step(layer)
                    for t in range(TT):
                        cols = probs[:, i % 2, t * 256:(t + 1) * 256]
                        ins = nc.vector.tensor_scalar(cols, cols, denom[:, t, i:i + 1], None, ALU.mult)
                    ins.then_inc(probs_scaled, 1)

                def o_lo(h):
                    dve.wait_ge(o_hi_ready, layer * CROSS_HEADS + h + 1)
                    nc.vector.tensor_tensor(pair[:, 2 * h:2 * h + 2, SEQ:2 * SEQ],
                                            ps[:, ACC[h], :].rearrange("p (c n) -> p c n", c=2),
                                            pair[:, 2 * h:2 * h + 2, 0:SEQ].bitcast(F32), ALU.subtract).then_inc(o_lo_ready, 1)

                head_max(12)
                head_max(13)
                scale_probs(12)
                head_max(14)
                scale_probs(13)
                o_lo(0)
                head_max(15)
                scale_probs(14)
                o_lo(1)
                scale_probs(15)
                o_lo(2)
                o_lo(3)
                split_lo(layer, 61)
                split_lo(layer, 62)
                split_lo(layer, 63)
                add_residual(layer, 2, 1.0)
                scale_rows(layer, 4)
                turn_pairs(layer, 4, "ffn2")
                ffn(layer, 1, U_FFN2)
                add_residual(layer, 3, 0.5)
                assert steps[0] == N_DVE, steps

            dve.wait_ge(last_rstd, 1)
            dve.wait_ge(gain_landed, 16)
            for t in range(TT):
                nc.vector.scalar_tensor_tensor(out=xn[:, t, :], in0=resid[:, t, :], scalar=rstd[:, t:t + 1],
                                               in1=y[:, 0, :], op0=ALU.mult, op1=ALU.mult).then_inc(result_ready, 1)

        @block.tensor
        def _(pe):
            def unit_split(layer, pos, turn=0):
                pe.wait_ge(lo_ready, layer * UNITS + turn * SLOTS + pos + 1 + CREDIT)

            def token_major(layer, pos, source, banks, ready=None, first_tile=None, turn=0, before=None):
                for half in range(2):
                    p = pos + half
                    s = slot_of(p)
                    unit_split(layer, p, turn)
                    whi = w_hi[:, s, :].rearrange("p (k n) -> p k n", k=4)
                    wlo = w_lo[:, s, :].rearrange("p (k n) -> p k n", k=4)
                    for t in range(TT):
                        for kk in range(4):
                            k = 4 * half + kk
                            if ready and t == 0 and kk % 2 == 0:
                                ready(k // 2)
                            if before and half == 0 and kk == 0:
                                before(t)
                            hi = source[:, k, t * P:(t + 1) * P]
                            lo = source[:, k, SEQ + t * P:SEQ + (t + 1) * P]
                            o = ps[:, banks[t], :]
                            nc.tensor.matmul(o, hi, whi[:, kk, :], start=(k == 0), stop=False)
                            nc.tensor.matmul(o, hi, wlo[:, kk, :], start=False, stop=False)
                            ins = nc.tensor.matmul(o, lo, whi[:, kk, :], start=False, stop=(k == KD - 1))
                        if half == 1 and t == 0 and first_tile:
                            ins.then_inc(first_tile, 1)
                    ins.then_inc(unit_used, 1)

            def accumulate(layer, pos, source, k0, first, last, turn=0, before=None):
                s = slot_of(pos)
                unit_split(layer, pos, turn)
                whi = w_hi[:, s, :].rearrange("p (k n) -> p k n", k=2)
                wlo = w_lo[:, s, :].rearrange("p (k n) -> p k n", k=2)
                for t in range(TT):
                    for kk in range(2):
                        hi = source[:, k0 + kk, t * P:(t + 1) * P]
                        lo = source[:, k0 + kk, SEQ + t * P:SEQ + (t + 1) * P]
                        for a, w, start, stop in ((hi, whi, True, False), (hi, wlo, False, False), (lo, whi, False, True)):
                            for c in range(2):
                                ins = nc.tensor.matmul(ps[:, ACC[2 * t + c], :], a, w[:, kk, c * 512:(c + 1) * 512],
                                                       start=first and kk == 0 and start, stop=last and kk == 1 and stop)
                    if last and t == 0:
                        ins.then_inc(acc_ready, 1)
                ins.then_inc(unit_used, 1)

            def feature_major(layer, pos, source, bank, ready=None):
                s = slot_of(pos)
                unit_split(layer, pos)
                whi = w_hi[:, s, :].rearrange("p (k n) -> p k n", k=KD)
                wlo = w_lo[:, s, :].rearrange("p (k n) -> p k n", k=KD)
                for c in range(2):
                    o = ps[:, bank, c * SEQ:(c + 1) * SEQ]
                    f = slice(c * P, (c + 1) * P)
                    for k in range(KD):
                        if ready and c == 0 and k % 2 == 0:
                            ready(k // 2)
                        nc.tensor.matmul(o, whi[:, k, f], source[:, k, 0:SEQ], start=(k == 0), stop=False)
                        nc.tensor.matmul(o, wlo[:, k, f], source[:, k, 0:SEQ], start=False, stop=False)
                        ins = nc.tensor.matmul(o, whi[:, k, f], source[:, k, SEQ:2 * SEQ], start=False, stop=(k == KD - 1))
                ins.then_inc(unit_used, 1)

            def turn_rows(layer, n):
                pe.wait_ge(xn_ready, (layer * N_NORM + n) * TT + TT)
                for kp in range(KD // 2):
                    for c in range(2):
                        k = 2 * kp + c
                        for t in range(TT):
                            ins = nc.tensor.transpose(ps[:, XB[kp], c * SEQ + t * P:c * SEQ + (t + 1) * P],
                                                      xn[:, t, k * P:(k + 1) * P], ident)
                    ins.then_inc(xn_turned, 1)

            def pair_ready(layer, n):
                return lambda kp: pe.wait_ge(pair_lo_ready, (layer * N_NORM + n) * 4 + kp + 1)

            def turn_hidden(layer, f, it):
                pe.wait_ge(hid_ready, layer * N_GU + (f * FFN_STEPS + it) * TT + TT)
                for c in range(2):
                    for t in range(TT):
                        ins = nc.tensor.transpose(ps[:, TP[0], c * SEQ + t * P:c * SEQ + (t + 1) * P],
                                                  hid[:, t, c * P:(c + 1) * P], ident)
                ins.then_inc(hid_turned, 1)

            def ffn(layer, f, first, ready):
                def free(it):
                    return lambda t: pe.wait_ge(hid_ready, layer * N_GU + (f * FFN_STEPS + it - 1) * TT + t + 1)

                def hidden_ready(it):
                    pe.wait_ge(hid_lo_ready, layer * N_HT + f * FFN_STEPS + it + 1)

                token_major(layer, first, pair, GU, ready, gate_up_ready)
                turn_hidden(layer, f, 0)
                token_major(layer, first + 2, pair, GU, None, gate_up_ready, 0, free(1))
                hidden_ready(0)
                accumulate(layer, first + 4, hid_pair, 0, True, False)
                turn_hidden(layer, f, 1)
                with pe.Fori(1, FFN_STEPS - 1) as turn:
                    token_major(layer, first + 2, pair, GU, None, gate_up_ready, turn, free(turn + 1))
                    hidden_ready(turn)
                    accumulate(layer, first + 4, hid_pair, 0, False, False, turn)
                    turn_hidden(layer, f, turn + 1)
                hidden_ready(FFN_STEPS - 1)
                accumulate(layer, first + FFN_UNITS - 1, hid_pair, 0, False, True)

            def mem_keys(layer, i):
                feature_major(layer, U_CK[i], mem_pair, ACC[2 + KV_BANK[i]])

            def mem_values(layer, half):
                banks = [ACC[2 + KV_BANK[4 + t]] for t in range(TT)]
                token_major(layer, U_CV[half], mem_pair, banks)

            pe.sem_inc(unit_used, CREDIT)
            pe.wait_ge(consts_landed, 16)
            pe.wait_ge(hankel_landed, 16)
            pe.wait_ge(mem_squares, 1)
            for j in range(DEPTH * B_HEADS // 2):
                if j >= 4:
                    pe.wait_ge(bias_kept, j - 3)
                nc.tensor.matmul(ps[:, ACC[j % 4], :], flip, hankel[:, 2 * j:2 * j + 2, :].rearrange("p g n -> p (g n)"),
                                 start=True, stop=True).then_inc(flip_ready, 1)
            pe.wait_ge(mem_scaled, TT)
            for kp in range(KD // 2):
                for c in range(2):
                    k = 2 * kp + c
                    for t in range(TT):
                        ins = nc.tensor.transpose(ps[:, XB[kp], c * SEQ + t * P:c * SEQ + (t + 1) * P],
                                                  xn[:, t, k * P:(k + 1) * P], ident)
                ins.then_inc(mem_turned, 1)
            pe.wait_ge(mem_kept, KD // 2)

            with pe.Fori(0, DEPTH) as layer:
                turn_rows(layer, 0)
                ffn(layer, 0, U_FFN1, pair_ready(layer, 0))
                pe.wait_ge(mem_lo_ready, layer + 1)
                pe.wait_ge(resid_ready, layer * N_RESID + 2 + 2)
                mem_keys(layer, 0)
                mem_keys(layer, 1)
                turn_rows(layer, 1)

                feature_major(layer, U_XR, pair, ACC[0], pair_ready(layer, 1))
                feature_major(layer, U_GATE, pair, ACC[1])
                token_major(layer, U_V, pair, GU)
                pe.wait_ge(kv_kept, layer * N_KV + 2)
                feature_major(layer, U_AQK[0], pair, ACC[2])
                feature_major(layer, U_AQK[1], pair, ACC[3])
                pe.wait_ge(conv_ready, layer + 1)
                pe.wait_ge(xr_kept, layer + 1)
                pe.wait_ge(proj_kept, layer * (N_PROJ - 1) + 1)
                for g in range(2):
                    for c in range(LT):
                        w = small[:, S_RG + (2 * g + c) * P:S_RG + (2 * g + c + 1) * P]
                        ins = nc.tensor.matmul(ps[:, ACC[g], c * SEQ:(c + 1) * SEQ], w, conv_out[:, c, :], start=True, stop=True)
                ins.then_inc(gates_ready, 1)
                pe.wait_ge(proj_kept, layer * (N_PROJ - 1) + 5)
                for j in range(2):
                    ins = nc.tensor.matmul(ps[:, TP[j], :], rot_t, qk_a_raw[:, 2 * j:2 * j + 2, :].rearrange("p c n -> p (c n)"),
                                           start=True, stop=True)
                ins.then_inc(rope_turned, 1)

                def scores(i):
                    b = i % 2
                    if i < A_HEADS:
                        h = A_ORDER[i]
                        half, q, k = h // 3, qk_a[:, h % 3, :], qk_a[:, 3, :]
                        if i == 0:
                            pe.wait_ge(rope_ready, layer + 1)
                            pe.wait_ge(proj_kept, layer * (N_PROJ - 1) + 3)
                    else:
                        h = i - 6
                        half, q, k = h % 2, qk_b[:, h // 2, :], qk_b[:, 3 + h // 2, :]
                        if i == 6:
                            pe.wait_ge(proj_kept, layer * (N_PROJ - 1) + 8)
                    if i >= 2:
                        pe.wait_ge(max_ready, layer * N_HEADS + i - 1)
                    rows = slice(64 * half, 64 * half + 64)
                    nc.tensor.matmul(ps[:, GU[b], 0:128], q[rows, 0:128], k[rows, 0:128], start=True, stop=True)
                    nc.tensor.matmul(ps[:, GU[b], 128:384], q[rows, 128:256], k[rows, 0:256],
                                     start=True, stop=True).then_inc(scores_ready, 1)

                def turn_probs(i):
                    b = i % 2
                    if i < 12:
                        pe.wait_ge(probs_ready, layer * N_HEADS + i + 1)
                        parts = [(0, 0), (128, 128), (256, 256)]
                    else:
                        pe.wait_ge(probs_scaled, layer * CROSS_HEADS + i - 12 + 1)
                        parts = [(c * 256 + t * 128, t * 256 + c * 128) for c in range(2) for t in range(TT)]
                    if i >= 2:
                        pe.wait_ge(probs_t_kept, layer * N_HEADS + i - 1)
                    for to, at in parts:
                        ins = nc.tensor.transpose(ps[:, TP[b], to:to + 128], probs[:, b, at:at + 128], ident)
                    ins.then_inc(probs_turned, 1)

                def weigh_values(i):
                    b = i % 2
                    pe.wait_ge(probs_t_kept, layer * N_HEADS + i + 1)
                    if i == 0:
                        pe.wait_ge(gates_exp_ready, layer + 1)
                    if i == 6:
                        pe.wait_ge(y_kept, 3 * layer + 1)
                    h = col(i) if i < 6 else i - 6
                    v = slice(64 * (h // 3), 64 * (h // 3) + 64) if i < 6 else slice(128 + 64 * h, 192 + 64 * h)
                    cols = slice(64 * h, 64 * h + 64)
                    nc.tensor.matmul(ps[:, ACC[0], cols], probs_t[:, b, 0:128], v_ab[:, 0, v], start=True, stop=True)
                    nc.tensor.matmul(ps[:, ACC[1], cols], probs_t[:, b, 128:256], v_ab[:, 0, v], start=True, stop=False)
                    ins = nc.tensor.matmul(ps[:, ACC[1], cols], probs_t[:, b, 256:384], v_ab[:, 1, v], start=False, stop=True)
                    if i in (5, 11):
                        ins.then_inc(y_ready, 1)

                for i in range(12 + 2):
                    if i < 12:
                        scores(i)
                    if 1 <= i <= 12:
                        turn_probs(i - 1)
                    if i in (0, 2, 4):
                        j = i // 2
                        if j == 0:
                            pe.wait_ge(proj_kept, layer * (N_PROJ - 1) + 4)
                        if j == 1:
                            pe.wait_ge(proj_kept, layer * (N_PROJ - 1) + 5)
                        if j == 2:
                            pe.wait_ge(proj_kept, layer * (N_PROJ - 1) + 6)
                        feature_major(layer, U_BQK[j], pair, ACC[2 + j % 2])
                    if i == 7:
                        pe.wait_ge(proj_kept, layer * (N_PROJ - 1) + 7)
                        mem_keys(layer, 2)
                    if i == 9:
                        mem_keys(layer, 3)
                    if i == 10:
                        pe.wait_ge(y_lru_ready, layer + 1)
                        pe.wait_ge(kv_kept, layer * N_KV + 3)
                        for t in range(TT):
                            for c in range(LT):
                                ins = nc.tensor.transpose(ps[:, ACC[3], t * SEQ + c * P:t * SEQ + (c + 1) * P],
                                                          y_lru[:, c, t * P:(t + 1) * P], ident)
                        ins.then_inc(y_lru_turned, 1)
                    if i >= 2:
                        weigh_values(i - 2)

                pe.wait_ge(y_kept, 3 * layer + 2)
                pe.wait_ge(kv_kept, layer * N_KV + 4)
                mem_values(layer, 0)
                turn_rows(layer, 2)
                for j in range(4):
                    pair_ready(layer, 2)(j)
                    if j == 0:
                        pe.wait_ge(kv_kept, layer * N_KV + 6)
                    accumulate(layer, U_WOUT + j, pair, 2 * j, j == 0, j == 3)
                pe.wait_ge(resid_ready, layer * N_RESID + 2 + 4)
                mem_values(layer, 1)
                turn_rows(layer, 3)
                for j in range(4):
                    if j == 2:
                        pe.wait_ge(kv_kept, layer * N_KV + 8)
                    feature_major(layer, U_CQ + j, pair, ACC[j], pair_ready(layer, 3) if j == 0 else None)

                def cross_scores(h):
                    i = 12 + h
                    pe.wait_ge(cq_kept, layer * CROSS_HEADS + h + 1)
                    if h >= 2:
                        pe.wait_ge(probs_ready, layer * N_HEADS + i - 1)
                    for t in range(TT):
                        for k in (2 * h, 2 * h + 1):
                            ins = nc.tensor.matmul(ps[:, GU[i % 2], t * SEQ:(t + 1) * SEQ], cq[:, k, t * P:(t + 1) * P],
                                                   ck[:, k, :], start=(k % 2 == 0), stop=(k % 2 == 1))
                    ins.then_inc(scores_ready, 1)

                def weigh_cross(h):
                    b = h % 2
                    pe.wait_ge(probs_t_kept, layer * N_HEADS + 12 + h + 1)
                    for c in range(2):
                        for r in range(TT):
                            f = slice(h * 256 + c * P, h * 256 + (c + 1) * P)
                            ins = nc.tensor.matmul(ps[:, ACC[h], c * SEQ:(c + 1) * SEQ], cv[:, r, f],
                                                   probs_t[:, b, r * SEQ:(r + 1) * SEQ], start=(r == 0), stop=(r == 1))
                    ins.then_inc(o_ready, 1)

                cross_scores(0)
                cross_scores(1)
                turn_probs(12)
                cross_scores(2)
                turn_probs(13)
                weigh_cross(0)
                cross_scores(3)
                turn_probs(14)
                weigh_cross(1)
                turn_probs(15)
                weigh_cross(2)
                weigh_cross(3)
                for j in range(4):
                    if j == 0:
                        pe.wait_ge(o_lo_ready, (layer + 1) * CROSS_HEADS)
                    accumulate(layer, U_CO + j, pair, 2 * j, j == 0, j == 3)
                turn_rows(layer, 4)
                ffn(layer, 1, U_FFN2, pair_ready(layer, 4))


def _feature_columns(w):
    return w.reshape(KD, P, 256).transpose(1, 0, 2).reshape(1, P, UNIT)


def _token_columns(w):
    return w.reshape(2, 4, P, 512).transpose(0, 2, 1, 3).reshape(2, P, UNIT)


def _rows(w):
    return w.reshape(-1, 2, P, D).transpose(0, 2, 1, 3).reshape(-1, P, UNIT)


def _ffn_units(w_in, w_out):
    cols = [_token_columns(np.concatenate([w_in[:, 256 * i:256 * i + 256], w_in[:, D_FF + 256 * i:D_FF + 256 * i + 256]], 1))
            for i in range(FFN_STEPS)]
    rows = _rows(w_out)
    parts = [cols[0]]
    for i in range(1, FFN_STEPS):
        parts += [cols[i], rows[i - 1:i]]
    return parts + [rows[FFN_STEPS - 1:]]


def _layer_stream(a, l):
    w = a["w_in"][l]
    q_a, k_a, v_a, q_b, k_b, v_b, xr, gate = np.split(w, np.cumsum([384, 128, 128, 384, 384, 384, 256]), 1)
    heads = q_a.reshape(D, 2, 3, HD)
    q_a = heads.transpose(0, 2, 1, 3).reshape(D, 384)
    qk_a = np.concatenate([q_a, k_a], 1)
    qk_b = np.concatenate([q_b, k_b], 1)
    c_kv = a["w_ckv"][l]
    keys = [_feature_columns(c_kv[:, 256 * i:256 * i + 256]) for i in range(4)]
    values = [_token_columns(c_kv[:, D + 512 * i:D + 512 * i + 512]) for i in range(2)]
    parts = _ffn_units(a["ffn1_w_in"][l], a["ffn1_w_out"][l])
    parts += [keys[0], keys[1], _feature_columns(xr), _feature_columns(gate), _token_columns(np.concatenate([v_a, v_b], 1))]
    parts += [_feature_columns(qk_a[:, 256 * i:256 * i + 256]) for i in range(2)]
    parts += [_feature_columns(qk_b[:, 256 * i:256 * i + 256]) for i in range(3)]
    parts += [keys[2], keys[3], values[0], _rows(a["w_out"][l]), values[1]]
    parts += [_feature_columns(a["w_cq"][l][:, 256 * i:256 * i + 256]) for i in range(4)]
    parts += [_rows(a["w_co"][l])]
    return np.concatenate(parts + _ffn_units(a["ffn2_w_in"][l], a["ffn2_w_out"][l]), 0)


def _small(a, l):
    def cols(v):
        return v.reshape(-1, P).T
    parts = [cols(a[n][l]) for n in ("ffn1_norm", "mix_norm", "group_norm", "cross_norm", "mem_norm", "ffn2_norm")]
    parts += [cols(a["conv_w"][l].reshape(-1)), cols(a["conv_b"][l]), cols(a["rg_a_b"][l]), cols(a["rg_x_b"][l]),
              cols(a["lru_lambda"][l]), np.broadcast_to(a["attn_sinks"][l], (P, A_HEADS))]
    for name in ("rg_a_w", "rg_x_w"):
        for c in range(LT):
            blocks = np.zeros((P, P), np.float32)
            blocks[:64, :64] = a[name][l, 2 * c]
            blocks[64:, 64:] = a[name][l, 2 * c + 1]
            parts.append(blocks)
    return np.concatenate(parts, 1)


def _constants():
    c = np.zeros((P, CONSTS), np.float32)
    c[:, C_ID:C_ID + P] = np.eye(P)
    c[:, C_FLIP:C_FLIP + P] = np.eye(P)[::-1]
    angle = np.arange(SEQ, dtype=np.float32)[:, None] * (
        np.float32(THETA) ** (-np.arange(0, ROT, 2, dtype=np.float32) / np.float32(ROT)))[None, :]
    c[:, C_COS:C_COS + SEQ] = 1.0
    for head in (0, HD):
        for i in range(ROT // 2):
            lo_, hi_ = head + i, head + i + ROT // 2
            c[hi_, C_ROT + lo_] = -1.0
            c[lo_, C_ROT + hi_] = 1.0
            for r in (lo_, hi_):
                c[r, C_COS:C_COS + SEQ] = np.cos(angle[:, i])
                c[r, C_SIN:C_SIN + SEQ] = np.sin(angle[:, i])
    chunk = np.arange(256)[None, :] // CHUNK - 2
    own = np.arange(P)[:, None] // CHUNK
    c[:, C_MASK:C_MASK + 256] = np.where((chunk <= own) & (chunk >= own - 1), 0.0, NEG)
    return c


def kernel(**inputs):
    import concourse.bacc as _bacc
    from concourse.bass_utils import run_bass_kernel_spmd as _run

    a = {n: np.ascontiguousarray(v) for n, v in inputs.items()}
    arrays = {
        "x": a["x"], "mem": a["mem"],
        "stream": np.concatenate([_layer_stream(a, l) for l in range(DEPTH)], 0),
        "small": np.stack([_small(a, l) for l in range(DEPTH)]),
        "rel": np.ascontiguousarray(a["rel_bias"][:, :, ::-1]),
        "final_norm": a["final_norm"],
        "constants": _constants(),
    }
    nc = _bacc.Bacc("TRN2", target_bir_lowering=False, num_devices=1)
    args = [nc.dram_tensor(f"in_{n}", v.shape, F32, kind="ExternalInput").ap() for n, v in arrays.items()]
    out = nc.dram_tensor("out_0", (1, SEQ, D), F32, kind="ExternalOutput").ap()
    trunk_kernel(nc, *args, out)
    r = _run(nc, [{f"in_{n}": v for n, v in arrays.items()}], core_ids=[0])
    return r.results[0]["out_0"]
```

```python
from contextlib import ExitStack

import numpy as np

import concourse.bass as bass
from concourse import mybir

F32 = mybir.dt.float32
F32R = mybir.dt.float32r
ALU = mybir.AluOpType
ACT = mybir.ActivationFunctionType
AX_X = mybir.AxisListType.X

P = 128
D = 1024
SEQ = 256
DEPTH = 2
TT = SEQ // P
KD = D // P
CHUNK = 64
HD = 64
LRU_W = 256
LT = LRU_W // P
A_HEADS = B_HEADS = 6
REL_CLIP = 256
ROT = 16
THETA = 500000.0
CROSS_HEADS = 4
D_FF = 2816
EPS = 1e-6
NEG = -1e30
GELU_CUBE = 0.044715
GELU_SCALE = float(np.sqrt(2.0 / np.pi))

UNIT = 2048
SLOTS = 3
FFN_STEPS = D_FF // 256
FFN_UNITS = 3 * FFN_STEPS
U_FFN1 = 0
U_CK = [33, 43, 44, 45]
U_V = 34
U_XR, U_GATE = 36, 37
U_AQK = [38, 39]
U_BQK = [40, 41, 42]
U_CV = [46, 52]
U_WOUT = 48
U_CQ = 54
U_CO = 58
U_FFN2 = 62
UNITS = U_FFN2 + FFN_UNITS
SLOT_USES = [(UNITS - s + SLOTS - 1) // SLOTS for s in range(SLOTS)]

S_CONVW, S_CONVB, S_BA, S_BX, S_LAM, S_SINK, S_RG = 0, 8, 10, 12, 14, 16, 22
SMALL = S_RG + 4 * P
C_ID, C_ROT, C_COS, C_SIN, C_MASK = 0, 128, 256, 512, 768
CONSTS = C_MASK + 256

ACC = [0, 1, 2, 3]
GU = [4, 5]
TP = [6, 7]
XB = GU + TP
KV_BANK = [ACC[0], ACC[3], ACC[2], ACC[3],
           ACC[2], ACC[3], ACC[0], ACC[1]]
CQ_BANK = [ACC[2], ACC[3], ACC[0], ACC[1]]

A_ORDER = [0, 3, 1, 4, 2, 5]

FFN1, MEM, MIX, GROUP, CROSS, FFN2 = range(6)
GROUPS = ((0, 384), (384, 768), (768, 1024))

N_NORM = 6
N_RESID = 4 * TT
N_GU = 2 * FFN_STEPS * TT
N_HT = 2 * FFN_STEPS
N_KV = 8
N_PROJ = 8
N_HEADS = A_HEADS + B_HEADS + CROSS_HEADS
N_Y = 4
N_DVE = 101
CREDIT = 3


def col(i):
    return A_ORDER[i] if i < A_HEADS else i


def slot_of(pos):
    return pos % SLOTS


def prior_unit(pos):
    if pos >= SLOTS:
        return pos - SLOTS
    last = max(q for q in range(UNITS) if q % SLOTS == pos % SLOTS)
    return last - UNITS


def trunk_kernel(nc, x, mem, stream, small_dram, gains_dram, rel_dram, consts_dram, out):
    with ExitStack() as ctx:
        def sb(name, shape, dt=F32):
            return ctx.enter_context(nc.sbuf_tensor(name, shape, dt))

        def sem(name):
            return ctx.enter_context(nc.semaphore(name))

        raw = sb("raw", [P, SLOTS, UNIT])
        w_hi = sb("w_hi", [P, SLOTS, UNIT], F32R)
        w_lo = sb("w_lo", [P, SLOTS, UNIT], F32R)
        resid = sb("resid", [P, TT, D])
        xn = sb("xn", [P, TT, D])
        pair = sb("pair", [P, KD, 2 * SEQ], F32R)
        gain_row = sb("gain_row", [P, 2, D])
        mem_pair = sb("mem_pair", [P, KD, 2 * SEQ], F32R)
        hid_pair = sb("hid_pair", [P, 2, 2 * SEQ], F32R)
        last_hid_pair = sb("last_hid_pair", [P, 2, 2 * SEQ], F32R)
        ffn_tmp = sb("ffn_tmp", [P, 1040])
        ck = sb("ck", [P, KD, SEQ])
        cv = sb("cv", [P, TT, D])
        y = sb("y", [P, TT, D])
        probs = sb("probs", [P, 2, 512])
        probs_t = sb("probs_t", [P, 2, 512])
        mix = sb("mix", [P, 4608])
        bias = sb("bias", [P, B_HEADS * 256])
        consts = sb("consts", [P, CONSTS])
        small = sb("small", [P, SMALL])
        sums = sb("sums", [P, TT, 3])
        rstd = sb("rstd", [P, TT, 3])
        expo = sb("expo", [P, 3])
        eps = sb("eps", [P, 3])
        row_max = sb("row_max", [P, TT, N_HEADS])
        neg_max = sb("neg_max", [P, TT, N_HEADS])
        denom = sb("denom", [P, TT, N_HEADS])
        sink_exp = sb("sink_exp", [P, TT, A_HEADS])
        sp = sb("sp", [P, 32])
        ps = ctx.enter_context(nc.psum_tensor("ps", [P, 8, 512], F32))

        o_pair = mem_pair
        silu = ffn_tmp[:, 0:512].rearrange("p (t n) -> p t n", t=2)
        hid = ffn_tmp[:, 512:1024].rearrange("p (t n) -> p t n", t=2)
        conv_in = ffn_tmp[:, 0:518].rearrange("p (c n) -> p c n", c=LT)
        conv_out = ffn_tmp[:, 518:1030].rearrange("p (c n) -> p c n", c=LT)
        conv_in_flat = ffn_tmp[:, 0:512]
        gate = xn[:, 0, 0:512]
        gelu = xn[:, 0, 512:1024]
        y_lru = xn[:, 1, 0:512].rearrange("p (c n) -> p c n", c=LT)
        lru = cv[:, :, :].rearrange("p t (a n) -> p (t a) n", a=2)
        qk_a_raw = mix[:, 0:1024].rearrange("p (j n) -> p j n", j=4)
        qk_a = mix[:, 1024:2048].rearrange("p (j n) -> p j n", j=4)
        qk_b = mix[:, 2048:3584].rearrange("p (j n) -> p j n", j=6)
        v_ab = mix[:, 3584:4608].rearrange("p (t n) -> p t n", t=TT)
        cq = mix[:, 0:2048].rearrange("p (k n) -> p k n", k=KD)
        ident = consts[:, C_ID:C_ID + P]
        rot_t = consts[:, C_ROT:C_ROT + P]
        cos = consts[:, C_COS:C_COS + SEQ]
        sin = consts[:, C_SIN:C_SIN + SEQ]
        window_mask = consts[:, C_MASK:C_MASK + 256]

        ident_landed, consts_landed, mem_landed, bias_landed = (
            sem("ident_landed"), sem("consts_landed"), sem("mem_landed"), sem("bias_landed"))
        x_landed = [sem("x_landed0"), sem("x_landed1")]
        gain_row_landed = [sem("gain_row_landed0"), sem("gain_row_landed1")]
        root_consts_ready = sem("root_consts_ready")
        raw_landed = [sem(f"raw_landed{s}") for s in range(SLOTS)]
        hi_ready, lo_ready, unit_used = sem("hi_ready"), sem("lo_ready"), sem("unit_used")
        small_landed = sem("small_landed")
        squares_ready, rstd_ready, xn_ready = sem("squares_ready"), sem("rstd_ready"), sem("xn_ready")
        xn_turned, pair_hi_ready, pair_lo_ready = sem("xn_turned"), sem("pair_hi_ready"), sem("pair_lo_ready")
        gate_up_ready, silu_ready, hid_ready = sem("gate_up_ready"), sem("silu_ready"), sem("hid_ready")
        hid_turned, hid_hi_ready, hid_lo_ready = sem("hid_turned"), sem("hid_hi_ready"), sem("hid_lo_ready")
        acc_ready, resid_ready = sem("acc_ready"), sem("resid_ready")
        kv_kept = sem("kv_kept")
        proj_kept, xr_kept = sem("proj_kept"), sem("xr_kept")
        conv_ready, gates_ready, gates_exp_ready = sem("conv_ready"), sem("gates_ready"), sem("gates_exp_ready")
        sig_ready, decay_ready, gain2_ready, root_ready = (
            sem("sig_ready"), sem("decay_ready"), sem("gain2_ready"), sem("root_ready"))
        cube_ready, gelu_tanh_ready, y_lru_ready, y_lru_turned = (
            sem("cube_ready"), sem("gelu_tanh_ready"), sem("y_lru_ready"), sem("y_lru_turned"))
        lam_ready, lam_exp_ready, decay_scale_ready = sem("lam_ready"), sem("lam_exp_ready"), sem("decay_scale_ready")
        rope_turned, rope_ready = sem("rope_turned"), sem("rope_ready")
        scores_ready, max_ready, probs_ready = sem("scores_ready"), sem("max_ready"), sem("probs_ready")
        probs_turned, probs_t_kept = sem("probs_turned"), sem("probs_t_kept")
        y_kept, cq_kept = sem("y_kept"), sem("cq_kept")
        y_ready, sink_ready, sink_exp_ready = sem("y_ready"), sem("sink_ready"), sem("sink_exp_ready")
        probs_scaled, o_ready, o_hi_ready, o_lo_ready = (
            sem("probs_scaled"), sem("o_ready"), sem("o_hi_ready"), sem("o_lo_ready"))
        dve_step, pool_step = sem("dve_step"), sem("pool_step")
        last_squares, last_rstd, result_ready, stored = (
            sem("last_squares"), sem("last_rstd"), sem("result_ready"), sem("stored"))

        block = ctx.enter_context(nc.Block())

        @block.sync
        def _(sp_eng):
            sp_eng.dma_start(resid[:, 0, :], x[0, 0:P, :]).then_inc(x_landed[0], 16)

            def load_unit(layer, pos, turn=0):
                s = slot_of(pos)
                sp_eng.wait_ge(lo_ready, layer * UNITS + turn * SLOTS + prior_unit(pos) + 1 + CREDIT)
                sp_eng.dma_start(
                    raw[:, s, :],
                    stream[bass.ds(layer * UNITS + turn * SLOTS + pos, 1), :, :].rearrange("a p n -> p (a n)"),
                ).then_inc(raw_landed[s], 16)

            def load_layer(layer, last):
                with sp_eng.Fori(0, UNITS // SLOTS - 1) as turn:
                    for s in range(SLOTS):
                        load_unit(layer, SLOTS + s, turn)
                for pos in range(UNITS // SLOTS * SLOTS, UNITS):
                    load_unit(layer, pos)
                if not last:
                    for pos in range(SLOTS):
                        load_unit(layer + 1, pos)

            load_unit(0, 0)
            sp_eng.dma_start(gain_row[:, 0, :], gains_dram[0:1, :].rearrange("a d -> (a d)").partition_broadcast(P))\
                  .then_inc(gain_row_landed[0], 16)
            sp_eng.dma_start(consts[:, 0:P], consts_dram[:, 0:P]).then_inc(ident_landed, 16)
            sp_eng.dma_start(resid[:, 1, :], x[0, P:2 * P, :]).then_inc(x_landed[1], 16)
            load_unit(0, 1)
            load_unit(0, 2)
            sp_eng.dma_start(consts[:, P:CONSTS], consts_dram[:, P:CONSTS]).then_inc(consts_landed, 16)
            with sp_eng.Fori(0, DEPTH - 1) as layer:
                load_layer(layer, False)
            load_layer(DEPTH - 1, True)
            for t in range(TT):
                sp_eng.wait_ge(result_ready, t + 1)
                sp_eng.dma_start(out[0, t * P:(t + 1) * P, :], xn[:, t, :]).then_inc(stored, 16)
            sp_eng.wait_ge(stored, 16 * TT)

        @block.gpsimd
        def _(pool):
            pool.memset(expo[:, :], -0.5).then_inc(root_consts_ready, 1)
            pool.memset(eps[:, :], EPS).then_inc(root_consts_ready, 1)
            pool.wait_ge(root_consts_ready, 2)

            def roots(before, t, width, signal):
                cols = rstd[:, t, 0:width]
                pool.tensor_tensor(cols, sums[:, t, 0:width], eps[:, 0:width], ALU.add).then_inc(pool_step, 1)
                pool.wait_ge(pool_step, before + 1)
                pool.tensor_tensor(cols, cols, expo[:, 0:width], ALU.pow).then_inc(signal, 1)

            with pool.Fori(0, DEPTH) as layer:
                for n in range(N_NORM):
                    for t in range(TT):
                        pool.wait_ge(squares_ready, (layer * N_NORM + n) * TT + t + 1)
                        roots((layer * N_NORM + n) * TT + t, t, 3 if n == GROUP else 1, rstd_ready)
            for t in range(TT):
                pool.wait_ge(last_squares, t + 1)
                roots(DEPTH * N_NORM * TT + t, t, 1, last_rstd)

        @block.scalar
        def _(act):
            def after_unit(layer, pos, turn=0):
                act.wait_ge(unit_used, layer * UNITS + turn * SLOTS + pos + 1 + CREDIT)

            def split_hi(layer, pos, turn=0):
                s = slot_of(pos)
                act.wait_ge(raw_landed[s], (layer * SLOT_USES[s] + turn + pos // SLOTS + 1) * 16)
                act.wait_ge(unit_used, layer * UNITS + turn * SLOTS + prior_unit(pos) + 1 + CREDIT)
                nc.scalar.activation(w_hi[:, s, :], raw[:, s, :], ACT.Copy).then_inc(hi_ready, 1)

            def squares(layer, n, t, source):
                ins = nc.scalar.activation(xn[:, t, :], source[:, t, :], ACT.Square, scale=D ** -0.5,
                                           accum_out=sums[:, t, 0:1])
                ins.then_inc(squares_ready, 1)

            def residual_squares(layer, n, use, t):
                act.wait_ge(resid_ready, layer * N_RESID + 2 * use + t + 1)
                squares(layer, n, t, resid)

            def keep_high(layer, n, t, target=pair, banks=XB):
                for b in range(2):
                    act.wait_ge(xn_turned, (layer * N_NORM + n) * 4 + 2 * t + b + 1)
                    nc.scalar.activation(target[:, 4 * b:4 * b + 4, t * P:(t + 1) * P],
                                         ps[:, banks[2 * t + b], :].rearrange("p (k n) -> p k n", k=4),
                                         ACT.Copy).then_inc(pair_hi_ready, 1)

            def load_gains(layer, n):
                act.dma_start(gain_row[:, n % 2, :],
                              gains_dram[bass.ds(layer * N_NORM + n, 1), :].rearrange("a d -> (a d)").partition_broadcast(P))\
                   .then_inc(gain_row_landed[n % 2], 16)

            def ffn_step(layer, f, it, last_unit, turn=0, tiles=range(TT)):
                for t in tiles:
                    if t == 0:
                        act.wait_ge(gate_up_ready, layer * 2 * FFN_STEPS + f * FFN_STEPS + it + 1)
                    else:
                        after_unit(layer, last_unit, turn)
                    nc.scalar.activation(silu[:, t, :], ps[:, GU[t], 0:256], ACT.Silu).then_inc(silu_ready, 1)

            def hid_hi(layer, f, it, target=hid_pair):
                act.wait_ge(hid_turned, layer * N_HT + f * FFN_STEPS + it + 1)
                nc.scalar.activation(target[:, :, 0:SEQ], ps[:, TP[0], :].rearrange("p (k n) -> p k n", k=2),
                                     ACT.Copy).then_inc(hid_hi_ready, 1)

            def ffn(layer, f, first, early=None, after_first=None):
                split_hi(layer, first + 2)
                if early:
                    early()
                ffn_step(layer, f, 0, first + 1, tiles=(0,))
                split_hi(layer, first + 3)
                ffn_step(layer, f, 0, first + 1, tiles=(1,))
                hid_hi(layer, f, 0)
                if after_first:
                    after_first()
                with act.Fori(0, FFN_STEPS - 2) as turn:
                    split_hi(layer, first + 4, turn)
                    ffn_step(layer, f, turn + 1, first + 3, turn)
                    split_hi(layer, first + 5, turn)
                    split_hi(layer, first + 6, turn)
                    hid_hi(layer, f, turn + 1)
                last = FFN_STEPS - 1
                split_hi(layer, first + 3 * last + 1)
                ffn_step(layer, f, last, first + 3 * last)
                split_hi(layer, first + 3 * last + 2)
                hid_hi(layer, f, last, last_hid_pair)
                if first + 3 * last + 3 < UNITS:
                    split_hi(layer, first + 3 * last + 3)

            def copy(out_ap, in_ap, signal):
                nc.scalar.activation(out_ap, in_ap, ACT.Copy).then_inc(signal, 1)

            def keep_kv(layer, i):
                order = [("k", 0), ("k", 1), ("k", 2), ("k", 3), ("v", 0), ("v", 1), ("v", 2), ("v", 3)]
                kind, j = order[i]
                after_unit(layer, U_CK[j] if kind == "k" else U_CV[j // 2] + 1)
                if kind == "k":
                    copy(ck[:, 2 * j:2 * j + 2, :], ps[:, KV_BANK[i], :].rearrange("p (c n) -> p c n", c=2), kv_kept)
                else:
                    t, half = j % 2, j // 2
                    copy(cv[:, t, half * 512:(half + 1) * 512], ps[:, KV_BANK[i], :], kv_kept)

            def head_probs(layer, i):
                act.wait_ge(max_ready, layer * N_HEADS + i + 1)
                b = i % 2
                if i < 12:
                    for t, lo_, hi_ in ((0, 0, 128), (1, 128, 384)):
                        ins = nc.scalar.activation(probs[:, b, lo_:hi_], probs[:, b, lo_:hi_], ACT.Exp,
                                                   bias=neg_max[:, t, col(i):col(i) + 1],
                                                   accum_out=denom[:, t, col(i):col(i) + 1])
                else:
                    act.wait_ge(probs_turned, layer * N_HEADS + i - 1)
                    for t in range(TT):
                        ins = nc.scalar.activation(probs[:, b, t * 256:(t + 1) * 256],
                                                   ps[:, GU[b], t * 256:(t + 1) * 256], ACT.Exp, scale=1.0 / 16,
                                                   bias=neg_max[:, t, col(i):col(i) + 1],
                                                   accum_out=denom[:, t, col(i):col(i) + 1])
                ins.then_inc(probs_ready, 1)

            def keep_probs_t(layer, i):
                n = 384 if i < 12 else 512
                act.wait_ge(probs_turned, layer * N_HEADS + i + 1)
                copy(probs_t[:, i % 2, 0:n], ps[:, TP[i % 2], 0:n], probs_t_kept)

            def o_hi(layer, h):
                act.wait_ge(o_ready, layer * CROSS_HEADS + h + 1)
                nc.scalar.activation(o_pair[:, 2 * h:2 * h + 2, 0:SEQ], ps[:, TP[h % 2], :].rearrange("p (c n) -> p c n", c=2),
                                     ACT.Copy).then_inc(o_hi_ready, 1)

            with act.Fori(0, DEPTH) as layer:
                act.wait_ge(resid_ready, layer * N_RESID + 1)
                squares(layer, FFN1, 0, resid)
                act.dma_start(y[:, :, :], mem.rearrange("b (t p) d -> p (b t) d", p=P)).then_inc(mem_landed, 16)
                act.dma_start(small[:, :], small_dram[bass.ds(layer, 1), :, :].rearrange("a p n -> p (a n)"))\
                   .then_inc(small_landed, 16)
                split_hi(layer, 0)
                keep_high(layer, FFN1, 0)
                act.wait_ge(resid_ready, layer * N_RESID + 2)
                squares(layer, FFN1, 1, resid)
                load_gains(layer, MEM)
                table = 2 * REL_CLIP + 1
                act.dma_start(bias[:, :].rearrange("p (h n) -> p h n", n=256),
                              bass.AP(rel_dram.tensor, layer * (B_HEADS * table) + REL_CLIP + P - 255,
                                      [[1, P], [table, B_HEADS], [1, 256]])).then_inc(bias_landed, 16)
                split_hi(layer, 1)
                keep_high(layer, FFN1, 1)

                def memory_squares():
                    act.wait_ge(mem_landed, (layer + 1) * 16)
                    for t in range(TT):
                        squares(layer, MEM, t, y)
                    load_gains(layer, MIX)

                def first_step_extras():
                    for t in range(TT):
                        keep_high(layer, MEM, t, mem_pair, ACC)
                    load_gains(layer, GROUP)

                ffn(layer, 0, U_FFN1, memory_squares, first_step_extras)
                split_hi(layer, 34)
                residual_squares(layer, MIX, 1, 0)
                split_hi(layer, 35)
                residual_squares(layer, MIX, 1, 1)
                keep_high(layer, MIX, 0)
                keep_kv(layer, 0)
                split_hi(layer, 36)
                keep_high(layer, MIX, 1)
                load_gains(layer, CROSS)
                act.wait_ge(lam_ready, layer + 1)
                nc.scalar.activation(sp[:, 4:6], sp[:, 2:4], ACT.Exp).then_inc(lam_exp_ready, 1)

                def keep_proj(i, out_ap, bank, shape=None):
                    after_unit(layer, (U_V + 1, U_V + 1, U_GATE, *U_AQK, *U_BQK)[i])
                    src = ps[:, bank, :]
                    copy(out_ap, src.rearrange("p (c n) -> p c n", c=2) if shape else src, proj_kept)

                keep_proj(0, v_ab[:, 0, :], GU[0])
                split_hi(layer, 37)
                keep_proj(1, v_ab[:, 1, :], GU[1])
                split_hi(layer, 38)
                split_hi(layer, 39)
                keep_proj(2, gate, ACC[1])
                split_hi(layer, 40)
                keep_proj(3, qk_a_raw[:, 0:2, :], ACC[2], 2)
                act.wait_ge(cube_ready, layer + 1)
                nc.scalar.activation(gelu, gelu, ACT.Tanh, scale=GELU_SCALE).then_inc(gelu_tanh_ready, 1)
                split_hi(layer, 41)
                keep_proj(4, qk_a_raw[:, 2:4, :], ACC[3], 2)
                act.wait_ge(gates_ready, layer + 1)
                act.wait_ge(decay_scale_ready, layer + 1)
                for g in range(2):
                    for c in range(LT):
                        ins = nc.scalar.activation(lru[:, g, c * SEQ:(c + 1) * SEQ], ps[:, ACC[g], c * SEQ:(c + 1) * SEQ],
                                                   ACT.Exp, scale=-1.0, bias=sp[:, 20 + 2 * g + c:21 + 2 * g + c])
                ins.then_inc(gates_exp_ready, 1)
                split_hi(layer, 42)
                keep_proj(5, qk_b[:, 0:2, :], ACC[2], 2)
                split_hi(layer, 43)

                def lru_decay():
                    act.wait_ge(sig_ready, layer + 1)
                    for c in range(LT):
                        for j, func, scale in ((2, ACT.Exp, sp[:, 18 + c:19 + c]), (3, ACT.Tanh, sp[:, 24 + c:25 + c])):
                            ins = nc.scalar.activation(lru[:, j, c * SEQ:(c + 1) * SEQ], lru[:, 0, c * SEQ:(c + 1) * SEQ],
                                                       func, scale=scale)
                    ins.then_inc(decay_ready, 1)

                for i in range(12 + 1):
                    if i == 1:
                        keep_proj(6, qk_b[:, 2:4, :], ACC[3], 2)
                        split_hi(layer, 44)
                    if i == 3:
                        keep_proj(7, qk_b[:, 4:6, :], ACC[2], 2)
                        split_hi(layer, 45)
                    if i in (5, 7, 9):
                        keep_kv(layer, (i - 3) // 2)
                        split_hi(layer, 46 + (i - 5) // 2)
                    if i >= 1:
                        keep_probs_t(layer, i - 1)
                    if i < 12:
                        head_probs(layer, i)
                    if i == 2:
                        lru_decay()
                    if i == 7:
                        act.wait_ge(gain2_ready, layer + 1)
                        nc.scalar.activation(lru[:, 3, :], lru[:, 3, :], ACT.Sqrt).then_inc(root_ready, 1)
                    if i == 6:
                        act.wait_ge(sink_ready, layer + 1)
                        nc.scalar.activation(sink_exp[:, :, :], sink_exp[:, :, :], ACT.Exp).then_inc(sink_exp_ready, 1)

                for t in range(TT):
                    act.wait_ge(y_kept, N_Y * layer + 3 + t)
                    for g, (lo_, hi_) in enumerate(GROUPS):
                        ins = nc.scalar.activation(xn[:, t, lo_:hi_], y[:, t, lo_:hi_], ACT.Square,
                                                   scale=(hi_ - lo_) ** -0.5, accum_out=sums[:, t, g:g + 1])
                    ins.then_inc(squares_ready, 1)
                keep_high(layer, GROUP, 0)
                keep_high(layer, GROUP, 1)
                split_hi(layer, 49)
                keep_kv(layer, 4)
                keep_kv(layer, 5)
                load_gains(layer, FFN2)
                split_hi(layer, 50)
                split_hi(layer, 51)
                split_hi(layer, 52)
                split_hi(layer, 53)
                residual_squares(layer, CROSS, 2, 0)
                residual_squares(layer, CROSS, 2, 1)
                split_hi(layer, 54)
                keep_high(layer, CROSS, 0)
                keep_high(layer, CROSS, 1)
                split_hi(layer, 55)
                keep_kv(layer, 6)
                keep_kv(layer, 7)
                split_hi(layer, 56)
                load_gains(layer, N_NORM)

                def keep_queries(u):
                    after_unit(layer, U_CQ + u)
                    copy(cq[:, 2 * u:2 * u + 2, :], ps[:, CQ_BANK[u], :].rearrange("p (c n) -> p c n", c=2), cq_kept)

                keep_queries(0)
                split_hi(layer, 57)
                head_probs(layer, 12)
                keep_queries(1)
                split_hi(layer, 58)
                head_probs(layer, 13)
                keep_probs_t(layer, 12)
                keep_queries(2)
                split_hi(layer, 59)
                o_hi(layer, 0)
                keep_probs_t(layer, 13)
                head_probs(layer, 14)
                o_hi(layer, 1)
                keep_queries(3)
                split_hi(layer, 60)
                keep_probs_t(layer, 14)
                head_probs(layer, 15)
                split_hi(layer, 61)
                o_hi(layer, 2)
                keep_probs_t(layer, 15)
                o_hi(layer, 3)
                residual_squares(layer, FFN2, 3, 0)
                split_hi(layer, 62)
                split_hi(layer, 63)
                keep_high(layer, FFN2, 0)
                residual_squares(layer, FFN2, 3, 1)
                keep_high(layer, FFN2, 1)
                ffn(layer, 1, U_FFN2)

            for t in range(TT):
                act.wait_ge(resid_ready, DEPTH * N_RESID + t + 1)
                nc.scalar.activation(xn[:, t, :], resid[:, t, :], ACT.Square, scale=D ** -0.5,
                                     accum_out=sums[:, t, 0:1]).then_inc(last_squares, 1)

        @block.vector
        def _(dve):
            steps = [0]

            def step(ins):
                ins.then_inc(dve_step, 1)
                steps[0] += 1

            def after_step(layer):
                dve.wait_ge(dve_step, layer * N_DVE + steps[0])

            def after_unit(layer, pos, turn=0):
                dve.wait_ge(unit_used, layer * UNITS + turn * SLOTS + pos + 1 + CREDIT)

            def split_lo(layer, pos, turn=0):
                s = slot_of(pos)
                dve.wait_ge(hi_ready, layer * UNITS + turn * SLOTS + pos + 1)
                nc.vector.tensor_tensor(w_lo[:, s, :], raw[:, s, :], w_hi[:, s, :].bitcast(F32),
                                        ALU.subtract).then_inc(lo_ready, 1)

            def scale_rows(layer, n, t, source=resid, target=xn):
                dve.wait_ge(rstd_ready, (layer * N_NORM + n) * TT + t + 1)
                if t == 0:
                    dve.wait_ge(gain_row_landed[n % 2], (layer * (N_NORM // 2) + n // 2 + 1) * 16)
                for g, (lo_, hi_) in enumerate(GROUPS if n == GROUP else ((0, D),)):
                    ins = nc.vector.scalar_tensor_tensor(out=target[:, t, lo_:hi_], in0=source[:, t, lo_:hi_],
                                                         scalar=rstd[:, t, g:g + 1], in1=gain_row[:, n % 2, lo_:hi_],
                                                         op0=ALU.mult, op1=ALU.mult)
                ins.then_inc(xn_ready, 1)

            def keep_low(layer, n, t, target=pair, banks=XB):
                for b in range(2):
                    dve.wait_ge(pair_hi_ready, (layer * N_NORM + n) * 4 + 2 * t + b + 1)
                    nc.vector.tensor_tensor(target[:, 4 * b:4 * b + 4, SEQ + t * P:SEQ + (t + 1) * P],
                                            ps[:, banks[2 * t + b], :].rearrange("p (k n) -> p k n", k=4),
                                            target[:, 4 * b:4 * b + 4, t * P:(t + 1) * P].bitcast(F32),
                                            ALU.subtract).then_inc(pair_lo_ready, 1)

            def add_residual(layer, use, scale, t):
                if t == 0:
                    dve.wait_ge(acc_ready, layer * (N_RESID // TT) + use + 1)
                else:
                    after_unit(layer, (U_FFN1 + FFN_UNITS - 1, U_WOUT + 3, U_CO + 3, U_FFN2 + FFN_UNITS - 1)[use])
                for c in range(2):
                    cols = slice(c * 512, (c + 1) * 512)
                    ins = nc.vector.scalar_tensor_tensor(out=resid[:, t, cols], in0=ps[:, ACC[2 * t + c], :],
                                                         scalar=scale, in1=resid[:, t, cols],
                                                         op0=ALU.mult, op1=ALU.add)
                ins.then_inc(resid_ready, 1)

            def ffn_step(layer, f, it, tiles=range(TT)):
                for t in tiles:
                    dve.wait_ge(silu_ready, layer * N_GU + (f * FFN_STEPS + it) * TT + t + 1)
                    nc.vector.tensor_tensor(hid[:, t, :], silu[:, t, :], ps[:, GU[t], 256:512],
                                            ALU.mult).then_inc(hid_ready, 1)

            def hid_lo(layer, f, it, target=hid_pair):
                dve.wait_ge(hid_hi_ready, layer * N_HT + f * FFN_STEPS + it + 1)
                nc.vector.tensor_tensor(target[:, :, SEQ:2 * SEQ], ps[:, TP[0], :].rearrange("p (k n) -> p k n", k=2),
                                        target[:, :, 0:SEQ].bitcast(F32), ALU.subtract).then_inc(hid_lo_ready, 1)

            def ffn(layer, f, first, early=None, after_first=None):
                split_lo(layer, first + 2)
                if early:
                    early()
                ffn_step(layer, f, 0, (0,))
                split_lo(layer, first + 3)
                ffn_step(layer, f, 0, (1,))
                hid_lo(layer, f, 0)
                if after_first:
                    after_first()
                with dve.Fori(0, FFN_STEPS - 2) as turn:
                    split_lo(layer, first + 4, turn)
                    ffn_step(layer, f, turn + 1)
                    split_lo(layer, first + 5, turn)
                    split_lo(layer, first + 6, turn)
                    hid_lo(layer, f, turn + 1)
                last = FFN_STEPS - 1
                split_lo(layer, first + 3 * last + 1)
                ffn_step(layer, f, last)
                split_lo(layer, first + 3 * last + 2)
                hid_lo(layer, f, last, last_hid_pair)
                if first + 3 * last + 3 < UNITS:
                    split_lo(layer, first + 3 * last + 3)

            def decay_scale(layer):
                lam = small[:, S_LAM:S_LAM + LT]
                dve.wait_ge(small_landed, (layer + 1) * 16)
                step(nc.vector.tensor_scalar(sp[:, 0:2], lam, -1.0, None, ALU.mult))
                step(nc.vector.tensor_scalar(sp[:, 20:24], small[:, S_BA:S_BA + 4], -1.0, None, ALU.mult))
                after_step(layer)
                nc.vector.tensor_tensor(sp[:, 2:4], sp[:, 0:2], lam, ALU.min).then_inc(lam_ready, 1)
                dve.wait_ge(lam_exp_ready, layer + 1)
                step(nc.vector.tensor_scalar(sp[:, 6:8], sp[:, 4:6], 2.0, None, ALU.add))
                after_step(layer)
                step(nc.vector.reciprocal(sp[:, 8:10], sp[:, 6:8]))
                after_step(layer)
                step(nc.vector.tensor_tensor(sp[:, 10:12], sp[:, 4:6], sp[:, 8:10], ALU.mult))
                after_step(layer)
                step(nc.vector.tensor_tensor(sp[:, 12:14], sp[:, 10:12], sp[:, 10:12], ALU.mult))
                after_step(layer)
                step(nc.vector.tensor_scalar(sp[:, 14:16], sp[:, 12:14], 1.0 / 17, None, ALU.mult))
                for odd in (15, 13, 11, 9, 7, 5, 3):
                    after_step(layer)
                    step(nc.vector.scalar_tensor_tensor(out=sp[:, 14:16], in0=sp[:, 14:16], scalar=1.0 / odd,
                                                        in1=sp[:, 12:14], op0=ALU.add, op1=ALU.mult))
                after_step(layer)
                step(nc.vector.scalar_tensor_tensor(out=sp[:, 14:16], in0=sp[:, 14:16], scalar=1.0,
                                                    in1=sp[:, 10:12], op0=ALU.add, op1=ALU.mult))
                step(nc.vector.tensor_scalar(sp[:, 16:18], sp[:, 0:2], 0.0, None, ALU.max))
                after_step(layer)
                step(nc.vector.scalar_tensor_tensor(out=sp[:, 14:16], in0=sp[:, 14:16], scalar=2.0,
                                                    in1=sp[:, 16:18], op0=ALU.mult, op1=ALU.add))
                after_step(layer)
                step(nc.vector.tensor_scalar(sp[:, 24:26], sp[:, 14:16], 8.0, None, ALU.mult))
                nc.vector.tensor_scalar(sp[:, 18:20], sp[:, 14:16], -8.0, None, ALU.mult).then_inc(decay_scale_ready, 1)

            def head_logits(layer, i):
                b = i % 2
                if i < A_HEADS:
                    table = window_mask
                else:
                    table = bias[:, (i - 6) * 256:(i - 5) * 256][:, ::-1]
                dve.wait_ge(scores_ready, layer * N_HEADS + i + 1)
                step(nc.vector.scalar_tensor_tensor(out=probs[:, b, 0:128], in0=ps[:, GU[b], 0:128], scalar=HD ** -0.5,
                                                    in1=table[:, 128:256], op0=ALU.mult, op1=ALU.add))
                step(nc.vector.scalar_tensor_tensor(out=probs[:, b, 128:384], in0=ps[:, GU[b], 128:384], scalar=HD ** -0.5,
                                                    in1=table, op0=ALU.mult, op1=ALU.add))
                after_step(layer)
                for t, lo_, hi_ in ((0, 0, 128), (1, 128, 384)):
                    step(nc.vector.reduce_max(row_max[:, t, col(i):col(i) + 1], probs[:, b, lo_:hi_], AX_X))
                after_step(layer)
                out_, in_ = neg_max[:, :, col(i)], row_max[:, :, col(i)]
                if i < A_HEADS:
                    sink = small[:, S_SINK + col(i):S_SINK + col(i) + 1]
                    nc.vector.tensor_scalar(out_, in_, sink, -1.0, ALU.max, ALU.mult).then_inc(max_ready, 1)
                else:
                    nc.vector.tensor_scalar(out_, in_, -1.0, None, ALU.mult).then_inc(max_ready, 1)

            def keep_y(layer, g):
                dve.wait_ge(y_ready, 2 * layer + g + 1)
                for t in range(TT):
                    scale = denom[:, t, 6 * g:6 * g + 6].unsqueeze(2).to_broadcast([P, 6, HD])
                    ins = nc.vector.tensor_tensor(
                        y[:, t, g * 384:(g + 1) * 384].rearrange("p (h d) -> p h d", h=6),
                        ps[:, ACC[t], 0:384].rearrange("p (h d) -> p h d", h=6), scale, ALU.mult)
                    if g == 1 or t == 1:
                        ins.then_inc(y_kept, 1)

            dve.sem_inc(lo_ready, CREDIT)

            with dve.Fori(0, DEPTH) as layer:
                scale_rows(layer, FFN1, 0)
                split_lo(layer, 0)
                keep_low(layer, FFN1, 0)
                scale_rows(layer, FFN1, 1)
                split_lo(layer, 1)
                keep_low(layer, FFN1, 1)

                def memory_rows():
                    for t in range(TT):
                        scale_rows(layer, MEM, t, y, y)

                def first_step_extras():
                    for t in range(TT):
                        keep_low(layer, MEM, t, mem_pair, ACC)

                ffn(layer, 0, U_FFN1, memory_rows, first_step_extras)
                split_lo(layer, 34)
                add_residual(layer, 0, 0.5, 0)
                add_residual(layer, 0, 0.5, 1)
                scale_rows(layer, MIX, 0)
                split_lo(layer, 35)
                keep_low(layer, MIX, 0)
                scale_rows(layer, MIX, 1)
                keep_low(layer, MIX, 1)
                dve.wait_ge(bias_landed, (layer + 1) * 16)
                step(nc.vector.memset(bias[0:64, :].rearrange("p (h n) -> p h n", n=256)[:, :, 0:64], NEG))
                split_lo(layer, 36)
                decay_scale(layer)
                split_lo(layer, 37)
                split_lo(layer, 38)

                step(nc.vector.memset(conv_in[:, :, 0:3], 0.0))
                after_unit(layer, U_XR)
                nc.vector.tensor_copy(conv_in[:, :, 3:3 + SEQ], ps[:, ACC[0], :].rearrange("p (c n) -> p c n", c=2))\
                         .then_inc(xr_kept, 1)
                after_step(layer)
                dve.wait_ge(xr_kept, layer + 1)
                for j in range(4):
                    for c in range(LT):
                        w = small[:, S_CONVW + 2 * j + c:S_CONVW + 2 * j + c + 1]
                        if j == 0:
                            step(nc.vector.tensor_scalar(conv_out[:, c, :], conv_in[:, c, 0:SEQ], w,
                                                         small[:, S_CONVB + c:S_CONVB + c + 1], ALU.mult, ALU.add))
                            continue
                        ins = nc.vector.scalar_tensor_tensor(out=conv_out[:, c, :], in0=conv_in[:, c, j:j + SEQ], scalar=w,
                                                             in1=conv_out[:, c, :], op0=ALU.mult, op1=ALU.add)
                        if j < 3 or c == 0:
                            step(ins)
                        else:
                            ins.then_inc(conv_ready, 1)
                    if j < 3:
                        after_step(layer)
                split_lo(layer, 39)
                dve.wait_ge(proj_kept, layer * N_PROJ + 3)
                step(nc.vector.tensor_tensor(gelu, gate, gate, ALU.mult))
                after_step(layer)
                step(nc.vector.tensor_scalar(gelu, gelu, GELU_CUBE, 1.0, ALU.mult, ALU.add))
                after_step(layer)
                nc.vector.tensor_tensor(gelu, gelu, gate, ALU.mult).then_inc(cube_ready, 1)
                split_lo(layer, 40)
                split_lo(layer, 41)
                dve.wait_ge(consts_landed, 16)
                dve.wait_ge(proj_kept, layer * N_PROJ + 5)
                over4 = lambda a: a.unsqueeze(1).to_broadcast([P, 4, SEQ])
                step(nc.vector.tensor_tensor(qk_a[:, :, :], qk_a_raw[:, :, :], over4(cos), ALU.mult))
                dve.wait_ge(gates_exp_ready, layer + 1)
                step(nc.vector.tensor_scalar(lru[:, 0, :], lru[:, 0, :], 1.0, None, ALU.add))
                after_step(layer)
                nc.vector.reciprocal(lru[:, 0, :], lru[:, 0, :]).then_inc(sig_ready, 1)
                dve.wait_ge(rope_turned, layer + 1)
                step(nc.vector.tensor_tensor(qk_a_raw[:, :, :], ps[:, TP[0]:TP[1] + 1, :].rearrange("p b (c n) -> p (b c) n", c=2),
                                             over4(sin), ALU.mult))
                after_step(layer)
                nc.vector.tensor_tensor(qk_a[:, :, :], qk_a[:, :, :], qk_a_raw[:, :, :], ALU.add).then_inc(rope_ready, 1)
                split_lo(layer, 42)

                def lru_input_gate(c):
                    cols = lru[:, 1, c * SEQ:(c + 1) * SEQ]
                    step(nc.vector.tensor_scalar(cols, cols, 1.0, None, ALU.add))
                    after_step(layer)
                    step(nc.vector.reciprocal(cols, cols))

                def lru_input_gain():
                    dve.wait_ge(decay_ready, layer + 1)
                    m = lru[:, 3, :]
                    square = conv_in_flat
                    step(nc.vector.tensor_tensor(square, lru[:, 2, :], lru[:, 2, :], ALU.mult))
                    after_step(layer)
                    nc.vector.scalar_tensor_tensor(out=m, in0=square, scalar=1.0, in1=m, op0=ALU.add,
                                                   op1=ALU.mult).then_inc(gain2_ready, 1)

                def lru_inputs():
                    after_step(layer)
                    step(nc.vector.tensor_tensor(lru[:, 1, :], lru[:, 1, :],
                                                 conv_out[:, :, :].rearrange("p c n -> p (c n)"), ALU.mult))
                    dve.wait_ge(gelu_tanh_ready, layer + 1)
                    step(nc.vector.scalar_tensor_tensor(out=gelu, in0=gelu, scalar=1.0, in1=gate, op0=ALU.add, op1=ALU.mult))

                def lru_scan():
                    dve.wait_ge(root_ready, layer + 1)
                    after_step(layer)
                    step(nc.vector.tensor_tensor(lru[:, 1, :], lru[:, 1, :], lru[:, 3, :], ALU.mult))
                    after_step(layer)
                    for c in range(LT):
                        cols = slice(c * SEQ, (c + 1) * SEQ)
                        step(nc.vector.tensor_tensor_scan(lru[:, 0, cols], lru[:, 2, cols], lru[:, 1, cols], 0.0,
                                                          ALU.mult, ALU.add))
                    after_step(layer)
                    nc.vector.scalar_tensor_tensor(out=xn[:, 1, 0:512], in0=gelu, scalar=0.5, in1=lru[:, 0, :],
                                                   op0=ALU.mult, op1=ALU.mult).then_inc(y_lru_ready, 1)

                for i in range(12 + 1):
                    if i < 12:
                        if i >= 2:
                            dve.wait_ge(probs_turned, layer * N_HEADS + i - 1)
                        head_logits(layer, i)
                    if i == 0:
                        split_lo(layer, 43)
                    if i in (1, 3, 5, 7):
                        split_lo(layer, 44 + (i - 1) // 2)
                    if i == 2:
                        lru_input_gate(0)
                    if i == 4:
                        lru_input_gate(1)
                    if i == 5:
                        dve.wait_ge(max_ready, layer * N_HEADS + 6)
                        for t in range(TT):
                            ins = nc.vector.tensor_tensor(sink_exp[:, t, :], neg_max[:, t, 0:6],
                                                          small[:, S_SINK:S_SINK + 6], ALU.add)
                        ins.then_inc(sink_ready, 1)
                    if i == 6:
                        lru_input_gain()
                    if i == 7:
                        dve.wait_ge(sink_exp_ready, layer + 1)
                        step(nc.vector.tensor_tensor(denom[:, :, 0:6], denom[:, :, 0:6], sink_exp[:, :, :], ALU.add))
                        after_step(layer)
                        step(nc.vector.reciprocal(denom[:, :, 0:6], denom[:, :, 0:6]))
                    if i == 8:
                        after_step(layer)
                        keep_y(layer, 0)
                        lru_inputs()
                    if i == 11:
                        lru_scan()
                dve.wait_ge(probs_ready, layer * N_HEADS + 12)
                step(nc.vector.reciprocal(denom[:, :, 6:12], denom[:, :, 6:12]))
                dve.wait_ge(y_lru_turned, layer + 1)
                nc.vector.tensor_copy(y[:, :, 768:1024], ps[:, GU[0], :].rearrange("p (t n) -> p t n", t=2)).then_inc(y_kept, 1)
                after_step(layer)
                keep_y(layer, 1)
                split_lo(layer, 48)

                scale_rows(layer, GROUP, 0, y)
                scale_rows(layer, GROUP, 1, y)
                keep_low(layer, GROUP, 0)
                keep_low(layer, GROUP, 1)
                for u in range(49, 54):
                    split_lo(layer, u)
                add_residual(layer, 1, 1.0, 0)
                add_residual(layer, 1, 1.0, 1)
                scale_rows(layer, CROSS, 0)
                scale_rows(layer, CROSS, 1)
                split_lo(layer, 54)
                keep_low(layer, CROSS, 0)
                keep_low(layer, CROSS, 1)
                split_lo(layer, 55)
                split_lo(layer, 56)
                split_lo(layer, 57)

                def head_max(i):
                    dve.wait_ge(scores_ready, layer * N_HEADS + i + 1)
                    step(nc.vector.reduce_max(row_max[:, :, i], ps[:, GU[i % 2], :].rearrange("p (t n) -> p t n", t=2), AX_X))
                    after_step(layer)
                    nc.vector.tensor_scalar(neg_max[:, :, i], row_max[:, :, i], -1.0 / 16, None, ALU.mult).then_inc(max_ready, 1)

                def scale_probs(i):
                    dve.wait_ge(probs_ready, layer * N_HEADS + i + 1)
                    step(nc.vector.reciprocal(denom[:, :, i], denom[:, :, i]))
                    after_step(layer)
                    for t in range(TT):
                        cols = probs[:, i % 2, t * 256:(t + 1) * 256]
                        ins = nc.vector.tensor_scalar(cols, cols, denom[:, t, i:i + 1], None, ALU.mult)
                    ins.then_inc(probs_scaled, 1)

                def o_lo(h):
                    dve.wait_ge(o_hi_ready, layer * CROSS_HEADS + h + 1)
                    nc.vector.tensor_tensor(o_pair[:, 2 * h:2 * h + 2, SEQ:2 * SEQ],
                                            ps[:, TP[h % 2], :].rearrange("p (c n) -> p c n", c=2),
                                            o_pair[:, 2 * h:2 * h + 2, 0:SEQ].bitcast(F32), ALU.subtract).then_inc(o_lo_ready, 1)

                head_max(12)
                scale_probs(12)
                split_lo(layer, 58)
                head_max(13)
                scale_probs(13)
                split_lo(layer, 59)
                o_lo(0)
                head_max(14)
                scale_probs(14)
                o_lo(1)
                head_max(15)
                split_lo(layer, 60)
                scale_probs(15)
                split_lo(layer, 61)
                o_lo(2)
                o_lo(3)
                add_residual(layer, 2, 1.0, 0)
                scale_rows(layer, FFN2, 0)
                split_lo(layer, 62)
                keep_low(layer, FFN2, 0)
                add_residual(layer, 2, 1.0, 1)
                split_lo(layer, 63)
                scale_rows(layer, FFN2, 1)
                keep_low(layer, FFN2, 1)
                ffn(layer, 1, U_FFN2)
                add_residual(layer, 3, 0.5, 0)
                add_residual(layer, 3, 0.5, 1)
                assert steps[0] == N_DVE, steps

            dve.wait_ge(gain_row_landed[0], (DEPTH * (N_NORM // 2) + 1) * 16)
            for t in range(TT):
                dve.wait_ge(last_rstd, t + 1)
                nc.vector.scalar_tensor_tensor(out=xn[:, t, :], in0=resid[:, t, :], scalar=rstd[:, t, 0:1],
                                               in1=gain_row[:, 0, :], op0=ALU.mult, op1=ALU.mult).then_inc(result_ready, 1)

        @block.tensor
        def _(pe):
            def unit_split(layer, pos, turn=0):
                pe.wait_ge(lo_ready, layer * UNITS + turn * SLOTS + pos + 1 + CREDIT)

            def token_quarter(layer, pos, source, banks, t, half, turn=0):
                p = pos + half
                s = slot_of(p)
                if t == 0:
                    unit_split(layer, p, turn)
                whi = w_hi[:, s, :].rearrange("p (k n) -> p k n", k=4)
                wlo = w_lo[:, s, :].rearrange("p (k n) -> p k n", k=4)
                for kk in range(4):
                    k = 4 * half + kk
                    hi = source[:, k, t * P:(t + 1) * P]
                    lo = source[:, k, SEQ + t * P:SEQ + (t + 1) * P]
                    o = ps[:, banks[t], :]
                    nc.tensor.matmul(o, hi, whi[:, kk, :], start=(k == 0), stop=False)
                    nc.tensor.matmul(o, hi, wlo[:, kk, :], start=False, stop=False)
                    ins = nc.tensor.matmul(o, lo, whi[:, kk, :], start=False, stop=(k == KD - 1))
                if t == TT - 1:
                    ins.then_inc(unit_used, 1)
                return ins

            def token_major(layer, pos, source, banks, norm=None, first_tile=None, turn=0, before=None, after_quarter=None):
                for t in range(TT):
                    if before:
                        before(t)
                    for half in range(2):
                        if norm is not None:
                            if (t, half) == ((1, 0) if norm == FFN2 else (0, 1)):
                                turn_rows(layer, norm, 1)
                            pair_ready(layer, norm, t, half)
                        ins = token_quarter(layer, pos, source, banks, t, half, turn)
                        if (t, half) == (0, 0) and after_quarter:
                            after_quarter()
                        if (t, half) == (0, 1) and first_tile:
                            ins.then_inc(first_tile, 1)

            def accumulate_tile(layer, pos, source, k0, t, first, last, turn=0):
                s = slot_of(pos)
                if t == 0:
                    unit_split(layer, pos, turn)
                whi = w_hi[:, s, :].rearrange("p (k n) -> p k n", k=2)
                wlo = w_lo[:, s, :].rearrange("p (k n) -> p k n", k=2)
                for kk in range(2):
                    hi = source[:, k0 + kk, t * P:(t + 1) * P]
                    lo = source[:, k0 + kk, SEQ + t * P:SEQ + (t + 1) * P]
                    for a, w, start, stop in ((hi, whi, True, False), (hi, wlo, False, False), (lo, whi, False, True)):
                        for c in range(2):
                            ins = nc.tensor.matmul(ps[:, ACC[2 * t + c], :], a, w[:, kk, c * 512:(c + 1) * 512],
                                                   start=first and kk == 0 and start, stop=last and kk == 1 and stop)
                if t == TT - 1:
                    ins.then_inc(unit_used, 1)
                elif last:
                    ins.then_inc(acc_ready, 1)

            def accumulate(layer, pos, source, k0, first, last, turn=0):
                for t in range(TT):
                    accumulate_tile(layer, pos, source, k0, t, first, last, turn)

            def feature_half(layer, pos, source, bank, c):
                s = slot_of(pos)
                if c == 0:
                    unit_split(layer, pos)
                whi = w_hi[:, s, :].rearrange("p (k n) -> p k n", k=KD)
                wlo = w_lo[:, s, :].rearrange("p (k n) -> p k n", k=KD)
                o = ps[:, bank, c * SEQ:(c + 1) * SEQ]
                f = slice(c * P, (c + 1) * P)
                for k in range(KD):
                    nc.tensor.matmul(o, whi[:, k, f], source[:, k, 0:SEQ], start=(k == 0), stop=False)
                    nc.tensor.matmul(o, wlo[:, k, f], source[:, k, 0:SEQ], start=False, stop=False)
                    ins = nc.tensor.matmul(o, whi[:, k, f], source[:, k, SEQ:2 * SEQ], start=False, stop=(k == KD - 1))
                if c == 1:
                    ins.then_inc(unit_used, 1)

            def feature_major(layer, pos, source, bank):
                for c in range(2):
                    feature_half(layer, pos, source, bank, c)

            def turn_rows(layer, n, t, source=xn, banks=XB):
                pe.wait_ge(xn_ready, (layer * N_NORM + n) * TT + t + 1)
                for b in range(2):
                    for kk in range(4):
                        k = 4 * b + kk
                        ins = nc.tensor.transpose(ps[:, banks[2 * t + b], kk * P:(kk + 1) * P],
                                                  source[:, t, k * P:(k + 1) * P], ident)
                    ins.then_inc(xn_turned, 1)

            def pair_ready(layer, n, t, b):
                pe.wait_ge(pair_lo_ready, (layer * N_NORM + n) * 4 + 2 * t + b + 1)

            def turn_hidden(layer, f, it):
                pe.wait_ge(hid_ready, layer * N_GU + (f * FFN_STEPS + it) * TT + TT)
                for c in range(2):
                    for t in range(TT):
                        ins = nc.tensor.transpose(ps[:, TP[0], c * SEQ + t * P:c * SEQ + (t + 1) * P],
                                                  hid[:, t, c * P:(c + 1) * P], ident)
                ins.then_inc(hid_turned, 1)

            def ffn(layer, f, first, norm):
                def free(it):
                    return lambda t: pe.wait_ge(hid_ready, layer * N_GU + (f * FFN_STEPS + it - 1) * TT + t + 1)

                def hidden_ready(it):
                    pe.wait_ge(hid_lo_ready, layer * N_HT + f * FFN_STEPS + it + 1)

                token_major(layer, first, pair, GU, norm, gate_up_ready)

                def on_the_way():
                    turn_hidden(layer, f, 0)
                    if f == 0:
                        for t in range(TT):
                            turn_rows(layer, MEM, t, y, ACC)

                token_major(layer, first + 2, pair, GU, None, gate_up_ready, 0, free(1), on_the_way)
                if f == 0:
                    pair_ready(layer, MEM, 1, 1)
                hidden_ready(0)
                accumulate(layer, first + 4, hid_pair, 0, True, False)
                turn_hidden(layer, f, 1)
                last = FFN_STEPS - 1
                with pe.Fori(1, last - 1) as turn:
                    token_major(layer, first + 2, pair, GU, None, gate_up_ready, turn, free(turn + 1))
                    hidden_ready(turn)
                    accumulate(layer, first + 4, hid_pair, 0, False, False, turn)
                    turn_hidden(layer, f, turn + 1)
                token_major(layer, first + 3 * last - 1, pair, GU, None, gate_up_ready, 0, free(last))
                hidden_ready(last - 1)
                accumulate_tile(layer, first + 3 * last + 1, hid_pair, 0, 0, False, False)
                turn_hidden(layer, f, last)
                accumulate_tile(layer, first + 3 * last + 1, hid_pair, 0, 1, False, False)
                hidden_ready(last)
                accumulate(layer, first + 3 * last + 2, last_hid_pair, 0, False, True)

            def mem_keys(layer, i, c):
                feature_half(layer, U_CK[i], mem_pair, KV_BANK[i], c)

            def mem_values(layer, i, t, half):
                token_quarter(layer, U_CV[i], mem_pair, KV_BANK[4 + 2 * i:6 + 2 * i], t, half)

            pe.sem_inc(unit_used, CREDIT)
            for t in range(TT):
                pe.wait_ge(x_landed[t], 16)
                pe.sem_inc(resid_ready, 1)
            pe.wait_ge(ident_landed, 16)

            with pe.Fori(0, DEPTH) as layer:
                turn_rows(layer, FFN1, 0)
                ffn(layer, 0, U_FFN1, FFN1)
                pe.wait_ge(resid_ready, layer * N_RESID + 2 + 1)
                mem_keys(layer, 0, 0)
                turn_rows(layer, MIX, 0)
                mem_keys(layer, 0, 1)
                token_major(layer, U_V, pair, GU, MIX)
                pe.wait_ge(kv_kept, layer * N_KV + 1)
                feature_major(layer, U_XR, pair, ACC[0])
                feature_major(layer, U_GATE, pair, ACC[1])
                feature_major(layer, U_AQK[0], pair, ACC[2])
                feature_major(layer, U_AQK[1], pair, ACC[3])
                pe.wait_ge(conv_ready, layer + 1)
                pe.wait_ge(xr_kept, layer + 1)
                pe.wait_ge(proj_kept, layer * N_PROJ + 3)
                for g in range(2):
                    for c in range(LT):
                        w = small[:, S_RG + (2 * g + c) * P:S_RG + (2 * g + c + 1) * P]
                        ins = nc.tensor.matmul(ps[:, ACC[g], c * SEQ:(c + 1) * SEQ], w, conv_out[:, c, :], start=True, stop=True)
                ins.then_inc(gates_ready, 1)
                pe.wait_ge(proj_kept, layer * N_PROJ + 4)
                feature_major(layer, U_BQK[0], pair, ACC[2])
                pe.wait_ge(consts_landed, 16)
                pe.wait_ge(proj_kept, layer * N_PROJ + 5)
                for j in range(2):
                    ins = nc.tensor.matmul(ps[:, TP[j], :], rot_t, qk_a_raw[:, 2 * j:2 * j + 2, :].rearrange("p c n -> p (c n)"),
                                           start=True, stop=True)
                ins.then_inc(rope_turned, 1)
                feature_half(layer, U_BQK[1], pair, ACC[3], 0)

                def scores(i):
                    b = i % 2
                    if i < A_HEADS:
                        h = A_ORDER[i]
                        half, q, k = h // 3, qk_a[:, h % 3, :], qk_a[:, 3, :]
                        if i == 0:
                            pe.wait_ge(rope_ready, layer + 1)
                            pe.wait_ge(proj_kept, layer * N_PROJ + 2)
                    else:
                        h = i - 6
                        half, q, k = h % 2, qk_b[:, h // 2, :], qk_b[:, 3 + h // 2, :]
                        if i == 6:
                            pe.wait_ge(proj_kept, layer * N_PROJ + 8)
                    if i >= 2:
                        pe.wait_ge(max_ready, layer * N_HEADS + i - 1)
                    rows = slice(64 * half, 64 * half + 64)
                    nc.tensor.matmul(ps[:, GU[b], 0:128], q[rows, 0:128], k[rows, 0:128], start=True, stop=True)
                    nc.tensor.matmul(ps[:, GU[b], 128:384], q[rows, 128:256], k[rows, 0:256],
                                     start=True, stop=True).then_inc(scores_ready, 1)

                def turn_probs(i):
                    b = i % 2
                    if i < 12:
                        pe.wait_ge(probs_ready, layer * N_HEADS + i + 1)
                        parts = [(0, 0), (128, 128), (256, 256)]
                    else:
                        pe.wait_ge(probs_scaled, layer * CROSS_HEADS + i - 12 + 1)
                        parts = [(c * 256 + t * 128, t * 256 + c * 128) for c in range(2) for t in range(TT)]
                        if i >= 14:
                            pe.wait_ge(o_lo_ready, layer * CROSS_HEADS + i - 13)
                    if i >= 2:
                        pe.wait_ge(probs_t_kept, layer * N_HEADS + i - 1)
                    for to, at in parts:
                        ins = nc.tensor.transpose(ps[:, TP[b], to:to + 128], probs[:, b, at:at + 128], ident)
                    ins.then_inc(probs_turned, 1)

                def weigh_values(i):
                    b = i % 2
                    pe.wait_ge(probs_t_kept, layer * N_HEADS + i + 1)
                    if i == 0:
                        pe.wait_ge(gates_exp_ready, layer + 1)
                    if i == 6:
                        pe.wait_ge(y_kept, N_Y * layer + 1)
                    h = col(i) if i < 6 else i - 6
                    v = slice(64 * (h // 3), 64 * (h // 3) + 64) if i < 6 else slice(128 + 64 * h, 192 + 64 * h)
                    cols = slice(64 * h, 64 * h + 64)
                    nc.tensor.matmul(ps[:, ACC[0], cols], probs_t[:, b, 0:128], v_ab[:, 0, v], start=True, stop=True)
                    nc.tensor.matmul(ps[:, ACC[1], cols], probs_t[:, b, 128:256], v_ab[:, 0, v], start=True, stop=False)
                    ins = nc.tensor.matmul(ps[:, ACC[1], cols], probs_t[:, b, 256:384], v_ab[:, 1, v], start=False, stop=True)
                    if i in (5, 11):
                        ins.then_inc(y_ready, 1)

                def filler(i):
                    if i == 0:
                        feature_half(layer, U_BQK[1], pair, ACC[3], 1)
                    elif i in (1, 2):
                        if i == 1:
                            pe.wait_ge(proj_kept, layer * N_PROJ + 6)
                        feature_half(layer, U_BQK[2], pair, ACC[2], i - 1)
                    elif i < 9:
                        key, c = (i - 3) // 2 + 1, (i - 3) % 2
                        if c == 0:
                            if key < 3:
                                pe.wait_ge(proj_kept, layer * N_PROJ + 6 + key)
                            else:
                                pe.wait_ge(kv_kept, layer * N_KV + 2)
                        mem_keys(layer, key, c)
                    elif i < 11:
                        mem_values(layer, 0, 0, i - 9)

                for i in range(12 + 2):
                    if i < 12:
                        scores(i)
                    if 1 <= i <= 12:
                        turn_probs(i - 1)
                    filler(i)
                    if i == 13:
                        pe.wait_ge(y_lru_ready, layer + 1)
                        pe.wait_ge(max_ready, layer * N_HEADS + 11)
                        for t in range(TT):
                            for c in range(LT):
                                ins = nc.tensor.transpose(ps[:, GU[0], t * SEQ + c * P:t * SEQ + (c + 1) * P],
                                                          y_lru[:, c, t * P:(t + 1) * P], ident)
                        ins.then_inc(y_lru_turned, 1)
                    if i >= 2:
                        weigh_values(i - 2)

                pe.wait_ge(kv_kept, layer * N_KV + 4)
                for b in range(2):
                    mem_values(layer, 0, 1, b)
                for t in range(TT):
                    turn_rows(layer, GROUP, t)
                for j in range(4):
                    for t in range(TT):
                        if j % 2 == 0:
                            pair_ready(layer, GROUP, t, j // 2)
                        if (j, t) == (0, 1):
                            pe.wait_ge(kv_kept, layer * N_KV + 6)
                        accumulate_tile(layer, U_WOUT + j, pair, 2 * j, t, j == 0, j == 3)
                pe.wait_ge(resid_ready, layer * N_RESID + 2 + 3)
                for b in range(2):
                    mem_values(layer, 1, 0, b)
                for b in range(2):
                    turn_rows(layer, CROSS, b)
                    mem_values(layer, 1, 1, b)
                pair_ready(layer, CROSS, 1, 1)

                def queries(j, c):
                    if j == 0:
                        pe.wait_ge(resid_ready, layer * N_RESID + 2 + 4)
                    if j == 2:
                        pe.wait_ge(kv_kept, layer * N_KV + 8)
                    feature_half(layer, U_CQ + j, pair, CQ_BANK[j], c)

                def cross_scores(h):
                    i = 12 + h
                    pe.wait_ge(cq_kept, layer * CROSS_HEADS + h + 1)
                    if h >= 2:
                        pe.wait_ge(probs_ready, layer * N_HEADS + i - 1)
                    for t in range(TT):
                        for k in (2 * h, 2 * h + 1):
                            ins = nc.tensor.matmul(ps[:, GU[i % 2], t * SEQ:(t + 1) * SEQ], cq[:, k, t * P:(t + 1) * P],
                                                   ck[:, k, :], start=(k % 2 == 0), stop=(k % 2 == 1))
                    ins.then_inc(scores_ready, 1)

                def weigh_cross(h):
                    b = h % 2
                    pe.wait_ge(probs_t_kept, layer * N_HEADS + 12 + h + 1)
                    for c in range(2):
                        for r in range(TT):
                            f = slice(h * 256 + c * P, h * 256 + (c + 1) * P)
                            ins = nc.tensor.matmul(ps[:, TP[b], c * SEQ:(c + 1) * SEQ], cv[:, r, f],
                                                   probs_t[:, b, r * SEQ:(r + 1) * SEQ], start=(r == 0), stop=(r == 1))
                    ins.then_inc(o_ready, 1)

                def cross_out(j, t):
                    if j == 0 and t == 0:
                        pe.wait_ge(cq_kept, (layer + 1) * CROSS_HEADS)
                    pe.wait_ge(o_lo_ready, layer * CROSS_HEADS + j + 1)
                    accumulate_tile(layer, U_CO + j, o_pair, 2 * j, t, j == 0, j == 3)

                queries(0, 0)
                queries(0, 1)
                queries(1, 0)
                cross_scores(0)
                queries(1, 1)
                queries(2, 0)
                cross_scores(1)
                turn_probs(12)
                queries(2, 1)
                weigh_cross(0)
                turn_probs(13)
                queries(3, 0)
                cross_scores(2)
                weigh_cross(1)
                queries(3, 1)
                turn_probs(14)
                cross_scores(3)
                cross_out(0, 0)
                cross_out(0, 1)
                weigh_cross(2)
                turn_probs(15)
                cross_out(1, 0)
                weigh_cross(3)
                cross_out(2, 0)
                cross_out(3, 0)
                cross_out(1, 1)
                cross_out(2, 1)
                turn_rows(layer, FFN2, 0)
                cross_out(3, 1)
                ffn(layer, 1, U_FFN2, FFN2)


def _feature_columns(w):
    return w.reshape(KD, P, 256).transpose(1, 0, 2).reshape(1, P, UNIT)


def _token_columns(w):
    return w.reshape(2, 4, P, 512).transpose(0, 2, 1, 3).reshape(2, P, UNIT)


def _rows(w):
    return w.reshape(-1, 2, P, D).transpose(0, 2, 1, 3).reshape(-1, P, UNIT)


def _ffn_units(w_in, w_out):
    cols = [_token_columns(np.concatenate([w_in[:, 256 * i:256 * i + 256], w_in[:, D_FF + 256 * i:D_FF + 256 * i + 256]], 1))
            for i in range(FFN_STEPS)]
    rows = _rows(w_out)
    parts = [cols[0]]
    for i in range(1, FFN_STEPS):
        parts += [cols[i], rows[i - 1:i]]
    return parts + [rows[FFN_STEPS - 1:]]


def _layer_stream(a, l):
    w = a["w_in"][l]
    q_a, k_a, v_a, q_b, k_b, v_b, xr, gate = np.split(w, np.cumsum([384, 128, 128, 384, 384, 384, 256]), 1)
    heads = q_a.reshape(D, 2, 3, HD)
    q_a = heads.transpose(0, 2, 1, 3).reshape(D, 384)
    qk_a = np.concatenate([q_a, k_a], 1)
    qk_b = np.concatenate([q_b, k_b], 1)
    c_kv = a["w_ckv"][l]
    keys = [_feature_columns(c_kv[:, 256 * i:256 * i + 256]) for i in range(4)]
    values = [_token_columns(c_kv[:, D + 512 * i:D + 512 * i + 512]) for i in range(2)]
    parts = _ffn_units(a["ffn1_w_in"][l], a["ffn1_w_out"][l])
    parts += [keys[0], _token_columns(np.concatenate([v_a, v_b], 1)), _feature_columns(xr), _feature_columns(gate)]
    parts += [_feature_columns(qk_a[:, 256 * i:256 * i + 256]) for i in range(2)]
    parts += [_feature_columns(qk_b[:, 256 * i:256 * i + 256]) for i in range(3)]
    parts += [keys[1], keys[2], keys[3], values[0], _rows(a["w_out"][l]), values[1]]
    parts += [_feature_columns(a["w_cq"][l][:, 256 * i:256 * i + 256]) for i in range(4)]
    parts += [_rows(a["w_co"][l])]
    return np.concatenate(parts + _ffn_units(a["ffn2_w_in"][l], a["ffn2_w_out"][l]), 0)


def _small(a, l):
    def cols(v):
        return v.reshape(-1, P).T
    parts = [cols(a["conv_w"][l].reshape(-1)), cols(a["conv_b"][l]), cols(a["rg_a_b"][l]), cols(a["rg_x_b"][l]),
              cols(a["lru_lambda"][l]), np.broadcast_to(a["attn_sinks"][l], (P, A_HEADS))]
    for name in ("rg_a_w", "rg_x_w"):
        for c in range(LT):
            blocks = np.zeros((P, P), np.float32)
            blocks[:64, :64] = a[name][l, 2 * c]
            blocks[64:, 64:] = a[name][l, 2 * c + 1]
            parts.append(blocks)
    return np.concatenate(parts, 1)


def _constants():
    c = np.zeros((P, CONSTS), np.float32)
    c[:, C_ID:C_ID + P] = np.eye(P)
    angle = np.arange(SEQ, dtype=np.float32)[:, None] * (
        np.float32(THETA) ** (-np.arange(0, ROT, 2, dtype=np.float32) / np.float32(ROT)))[None, :]
    c[:, C_COS:C_COS + SEQ] = 1.0
    for head in (0, HD):
        for i in range(ROT // 2):
            lo_, hi_ = head + i, head + i + ROT // 2
            c[hi_, C_ROT + lo_] = -1.0
            c[lo_, C_ROT + hi_] = 1.0
            for r in (lo_, hi_):
                c[r, C_COS:C_COS + SEQ] = np.cos(angle[:, i])
                c[r, C_SIN:C_SIN + SEQ] = np.sin(angle[:, i])
    chunk = np.arange(256)[None, :] // CHUNK - 2
    own = np.arange(P)[:, None] // CHUNK
    c[:, C_MASK:C_MASK + 256] = np.where((chunk <= own) & (chunk >= own - 1), 0.0, NEG)
    return c


def kernel(**inputs):
    import concourse.bacc as _bacc
    from concourse.bass_utils import run_bass_kernel_spmd as _run

    a = {n: np.ascontiguousarray(v) for n, v in inputs.items()}
    arrays = {
        "x": a["x"], "mem": a["mem"],
        "stream": np.concatenate([_layer_stream(a, l) for l in range(DEPTH)], 0),
        "small": np.stack([_small(a, l) for l in range(DEPTH)]),
        "gains": np.stack([a[n][l] for l in range(DEPTH) for n in (
            "ffn1_norm", "mem_norm", "mix_norm", "group_norm", "cross_norm", "ffn2_norm")] + [a["final_norm"]]),
        "rel": a["rel_bias"],
        "constants": _constants(),
    }
    nc = _bacc.Bacc("TRN2", target_bir_lowering=False, num_devices=1)
    args = [nc.dram_tensor(f"in_{n}", v.shape, F32, kind="ExternalInput").ap() for n, v in arrays.items()]
    out = nc.dram_tensor("out_0", (1, SEQ, D), F32, kind="ExternalOutput").ap()
    trunk_kernel(nc, *args, out)
    r = _run(nc, [{f"in_{n}": v for n, v in arrays.items()}], core_ids=[0])
    return r.results[0]["out_0"]
```
